# Optimizing a Trainium2 kernel written in Bass

```python
import jax, jax.numpy as jnp
from jax import lax
import numpy as np
import math

D_MODEL = 1024
BATCH = 1
SEQ = 512
DEPTH = 1

HEAD_DIM = 128
HEADS_PER_GROUP = 4
DILATION_GROUPS = ((128, 1), (512, 4), (2048, 16))
N_GROUPS = 3
ATT_WIDTH = HEADS_PER_GROUP * HEAD_DIM
QKV_WIDTH = N_GROUPS * ATT_WIDTH
BAND_BLOCK = 128
LRU_WIDTH = D_MODEL
LRU_BLOCKS = 16
LRU_BLOCK_DIM = LRU_WIDTH // LRU_BLOCKS
CONV_WIDTH = 4
LRU_C = 8.0
N_BRANCHES = 2
NORM_EPS = 1e-6
NEG_INF = -1e30
SPLIT_SIZES = (QKV_WIDTH, QKV_WIDTH, QKV_WIDTH, ATT_WIDTH, LRU_WIDTH, LRU_WIDTH, N_BRANCHES * D_MODEL)
IN_WIDTH = 3 * QKV_WIDTH + ATT_WIDTH + 2 * LRU_WIDTH + N_BRANCHES * D_MODEL


def rms_norm(x, gain):
    xf = x.astype(jnp.float32)
    y = xf * lax.rsqrt(jnp.mean(xf * xf, axis=-1, keepdims=True) + NORM_EPS)
    return (y * gain.astype(jnp.float32)).astype(x.dtype)

def dilated_window_group(q, k, v, window, dilation):
    B, S, H, Dh = q.shape
    span = window // dilation
    L = S // dilation
    n_blk = -(-L // BAND_BLOCK)
    Lp = n_blk * BAND_BLOCK

    def to_sub(t):
        t = t.astype(jnp.float32).reshape(B, L, dilation, H, Dh).transpose(0, 2, 1, 3, 4)
        return jnp.pad(t, ((0, 0), (0, 0), (0, Lp - L), (0, 0), (0, 0)))

    def band(t):
        t = jnp.pad(to_sub(t), ((0, 0), (0, 0), (BAND_BLOCK, 0), (0, 0), (0, 0)))
        t = t.reshape(B, dilation, n_blk + 1, BAND_BLOCK, H, Dh)
        return jnp.concatenate([t[:, :, :-1], t[:, :, 1:]], axis=3)

    qs = to_sub(q).reshape(B, dilation, n_blk, BAND_BLOCK, H, Dh)
    kb = band(k)
    vb = band(v)
    s = jnp.einsum('brnqhd,brnkhd->brnhqk', qs, kb) * (Dh ** -0.5)
    qi = jnp.arange(BAND_BLOCK)[:, None] + BAND_BLOCK
    ki = jnp.arange(2 * BAND_BLOCK)[None, :]
    dist = qi - ki
    key_pos = jnp.arange(n_blk)[:, None, None] * BAND_BLOCK + ki[None] - BAND_BLOCK
    valid = (dist >= 0) & (dist <= span) & (key_pos >= 0)
    s = jnp.where(valid[None, None, :, None], s, NEG_INF)
    m = jnp.max(s, axis=-1)
    p = jnp.exp(s - m[..., None])
    l = jnp.sum(p, axis=-1)
    m = jnp.swapaxes(m, -1, -2)
    l = jnp.swapaxes(l, -1, -2)
    o = jnp.einsum('brnhqk,brnkhd->brnqhd', p, vb) / l[..., None]

    def from_sub(t):
        t = t.reshape((B, dilation, Lp) + t.shape[4:])[:, :, :L]
        t = jnp.swapaxes(t, 1, 2)
        return t.reshape((B, S) + t.shape[3:])

    return from_sub(o), from_sub(m), from_sub(l)

def dilated_attention(q, k, v):
    B, S, _ = q.shape
    shp = (B, S, N_GROUPS, HEADS_PER_GROUP, HEAD_DIM)
    qg, kg, vg = q.reshape(shp), k.reshape(shp), v.reshape(shp)
    outs, maxes, dens = [], [], []
    for g, (window, dilation) in enumerate(DILATION_GROUPS):
        o, m, l = dilated_window_group(qg[:, :, g], kg[:, :, g], vg[:, :, g], window, dilation)
        outs.append(o)
        maxes.append(m)
        dens.append(l)
    o = jnp.stack(outs, 0)
    m = jnp.stack(maxes, 0)
    l = jnp.stack(dens, 0)
    wgt = l * jnp.exp(m - jnp.max(m, axis=0, keepdims=True))
    o = jnp.sum(wgt[..., None] * o, axis=0) / jnp.sum(wgt, axis=0)[..., None]
    return o.reshape(B, S, ATT_WIDTH).astype(q.dtype)

def causal_depthwise_conv(u, w, b):
    S = u.shape[1]
    up = jnp.pad(u, ((0, 0), (CONV_WIDTH - 1, 0), (0, 0)))
    y = b
    for j in range(CONV_WIDTH):
        y = y + up[:, CONV_WIDTH - 1 - j: CONV_WIDTH - 1 - j + S] * w[j]
    return y

def rg_lru(u, w_rg, b_rg, w_ig, b_ig, lru_lambda):
    B, S, _ = u.shape
    uf = u.astype(jnp.float32)
    ub = uf.reshape(B, S, LRU_BLOCKS, LRU_BLOCK_DIM)
    r = jax.nn.sigmoid(jnp.einsum('bshi,hij->bshj', ub, w_rg.astype(jnp.float32)).reshape(B, S, LRU_WIDTH) + b_rg.astype(jnp.float32))
    i = jax.nn.sigmoid(jnp.einsum('bshi,hij->bshj', ub, w_ig.astype(jnp.float32)).reshape(B, S, LRU_WIDTH) + b_ig.astype(jnp.float32))
    log_a = -LRU_C * r * jax.nn.softplus(-lru_lambda.astype(jnp.float32))
    a = jnp.exp(log_a)
    xin = jnp.sqrt(-jnp.expm1(2.0 * log_a)) * (i * uf)

    def combine(left, right):
        a1, b1 = left
        a2, b2 = right
        return a1 * a2, a2 * b1 + b2

    _, h = lax.associative_scan(combine, (a, xin), axis=1)
    return h.astype(u.dtype)

def hybrid_layer(x, c, w_mod, b_mod, g_pre, w_in, conv_w, conv_b, w_rg, b_rg, w_ig, b_ig,
                 lru_lambda, w_pa, w_pb, w_o, g_post):
    mod = jax.nn.silu(c) @ w_mod + b_mod
    shift, scale, gate = jnp.split(mod[:, None, :], 3, axis=-1)
    h = rms_norm(x, g_pre) * (1 + scale) + shift
    proj = h @ w_in
    split_at = [int(v) for v in np.cumsum(SPLIT_SIZES)[:-1]]
    q, k, v, g_att, u, g_lru, merge = jnp.split(proj, split_at, axis=-1)
    y_a = (dilated_attention(q, k, v) * jax.nn.silu(g_att)) @ w_pa
    u = causal_depthwise_conv(u, conv_w, conv_b)
    y_b = (rg_lru(u, w_rg, b_rg, w_ig, b_ig, lru_lambda) * jax.nn.silu(g_lru)) @ w_pb
    gate_a, gate_b = jnp.split(jax.nn.sigmoid(merge), N_BRANCHES, axis=-1)
    out = (gate_a * y_a + gate_b * y_b) @ w_o
    return x + gate * rms_norm(out, g_post)

def first_inputs(seed: int = 0) -> dict:
    key = jax.random.key(seed)
    ks = jax.random.split(key, 20)
    f32 = jnp.float32
    nrm = lambda k, shape, s: jax.random.normal(k, shape, f32) * s
    u = jax.random.uniform(ks[13], (DEPTH, LRU_WIDTH), f32, 0.9, 0.999)
    a_base = u ** (1.0 / LRU_C)
    lru_lambda = jnp.log(a_base) - jnp.log1p(-a_base)
    return {
        "x": nrm(ks[0], (BATCH, SEQ, D_MODEL), 1.0),
        "c": nrm(ks[1], (BATCH, D_MODEL), 1.0),
        "w_mod": nrm(ks[2], (DEPTH, D_MODEL, 3 * D_MODEL), 0.5 * D_MODEL ** -0.5),
        "b_mod": nrm(ks[3], (DEPTH, 3 * D_MODEL), 0.01),
        "g_pre": 1.0 + nrm(ks[4], (DEPTH, D_MODEL), 0.05),
        "w_in": nrm(ks[5], (DEPTH, D_MODEL, IN_WIDTH), D_MODEL ** -0.5),
        "conv_w": nrm(ks[6], (DEPTH, CONV_WIDTH, LRU_WIDTH), CONV_WIDTH ** -0.5),
        "conv_b": nrm(ks[7], (DEPTH, LRU_WIDTH), 0.01),
        "w_rg": nrm(ks[8], (DEPTH, LRU_BLOCKS, LRU_BLOCK_DIM, LRU_BLOCK_DIM), LRU_BLOCK_DIM ** -0.5),
        "b_rg": nrm(ks[9], (DEPTH, LRU_WIDTH), 0.01),
        "w_ig": nrm(ks[10], (DEPTH, LRU_BLOCKS, LRU_BLOCK_DIM, LRU_BLOCK_DIM), LRU_BLOCK_DIM ** -0.5),
        "b_ig": nrm(ks[11], (DEPTH, LRU_WIDTH), 0.01),
        "lru_lambda": lru_lambda,
        "w_pa": nrm(ks[14], (DEPTH, ATT_WIDTH, D_MODEL), ATT_WIDTH ** -0.5),
        "w_pb": nrm(ks[15], (DEPTH, LRU_WIDTH, D_MODEL), LRU_WIDTH ** -0.5),
        "w_o": nrm(ks[16], (DEPTH, D_MODEL, D_MODEL), D_MODEL ** -0.5),
        "g_post": 1.0 + nrm(ks[17], (DEPTH, D_MODEL), 0.05),
    }

def first_block(x, c, w_mod, b_mod, g_pre, w_in, conv_w, conv_b, w_rg, b_rg, w_ig, b_ig,
              lru_lambda, w_pa, w_pb, w_o, g_post):
    for layer in range(DEPTH):
        x = hybrid_layer(x, c, w_mod[layer], b_mod[layer], g_pre[layer], w_in[layer],
                         conv_w[layer], conv_b[layer], w_rg[layer], b_rg[layer],
                         w_ig[layer], b_ig[layer], lru_lambda[layer], w_pa[layer],
                         w_pb[layer], w_o[layer], g_post[layer])
    return x


DEPTH_2 = 2

GRID_W = 64
CTX_LEN = 256
D_MIX = D_MODEL
N_MIXERS = 4
GROUP_W = D_MIX // N_MIXERS
N_PARTS = 10
D_IN = N_PARTS * GROUP_W
CONV_A_K = 31
DIFF_HEADS = 4
DIFF_DQK = GROUP_W // (2 * DIFF_HEADS)
DIFF_DV = 2 * DIFF_DQK
ROPE_HALF = DIFF_DQK // 2
ROPE_BASE = 10000.0
Q_BLOCK = 128
CHUNK = 128
SG_GROUPS = 4
SG_DIM = GROUP_W // SG_GROUPS
CONV_D_K = 3
D_FF = 4 * D_MODEL
EPS = 1e-6


def rms_norm_2(x, g):
    xf = x.astype(jnp.float32)
    y = xf * lax.rsqrt(jnp.mean(xf * xf, axis=-1, keepdims=True) + EPS)
    return (y * g.astype(jnp.float32)).astype(x.dtype)

def layer_norm(x, g, b):
    xf = x.astype(jnp.float32)
    xc = xf - jnp.mean(xf, axis=-1, keepdims=True)
    y = xc * lax.rsqrt(jnp.mean(xc * xc, axis=-1, keepdims=True) + EPS)
    return (y * g.astype(jnp.float32) + b.astype(jnp.float32)).astype(x.dtype)

def modulate(h, shift, scale):
    return h * (1 + scale) + shift

def depthwise_conv(x, w):
    pad = w.shape[0] // 2
    return lax.conv_general_dilated(
        x, w[:, None, :].astype(x.dtype), window_strides=(1,), padding=[(pad, pad)],
        dimension_numbers=('NWC', 'WIO', 'NWC'), feature_group_count=x.shape[-1])

def axial_rope(rows, dtype):
    row = jnp.repeat(jnp.arange(rows, dtype=jnp.float32), GRID_W)
    col = jnp.tile(jnp.arange(GRID_W, dtype=jnp.float32), rows)
    inv = ROPE_BASE ** (-jnp.arange(0, ROPE_HALF, 2, dtype=jnp.float32) / ROPE_HALF)
    ang_r = row[:, None] * inv
    ang_c = col[:, None] * inv
    return (jnp.cos(ang_r)[:, None, :].astype(dtype), jnp.sin(ang_r)[:, None, :].astype(dtype),
            jnp.cos(ang_c)[:, None, :].astype(dtype), jnp.sin(ang_c)[:, None, :].astype(dtype))

def rotate_pairs(t, cos, sin):
    f = t.shape[-1] // 2
    t1, t2 = t[..., :f], t[..., f:]
    return jnp.concatenate([t1 * cos - t2 * sin, t1 * sin + t2 * cos], axis=-1)

def apply_axial_rope(t, rope):
    cos_r, sin_r, cos_c, sin_c = rope
    return jnp.concatenate([rotate_pairs(t[..., :ROPE_HALF], cos_r, sin_r),
                            rotate_pairs(t[..., ROPE_HALF:], cos_c, sin_c)], axis=-1)

def qk_heads(t, rope):
    b, n, _ = t.shape
    t = t.reshape(b, n, DIFF_HEADS, 2, DIFF_DQK)
    t1, t2 = t[..., 0, :], t[..., 1, :]
    if rope is not None:
        t1, t2 = apply_axial_rope(t1, rope), apply_axial_rope(t2, rope)
    return t1, t2

def v_heads(t):
    b, n, _ = t.shape
    return t.reshape(b, n, DIFF_HEADS, DIFF_DV)

def diff_attention(q1, q2, k1, k2, v, lam, lam_init, subln_g):
    b, n = q1.shape[:2]
    nb = n // Q_BLOCK
    scale = DIFF_DQK ** -0.5

    def blocks(t):
        return t.reshape(b, nb, Q_BLOCK, DIFF_HEADS, DIFF_DQK).transpose(1, 0, 2, 3, 4)

    def one_block(qs):
        qb1, qb2 = qs
        p1 = jax.nn.softmax(jnp.einsum('bqhd,bkhd->bhqk', qb1, k1).astype(jnp.float32) * scale, axis=-1)
        p2 = jax.nn.softmax(jnp.einsum('bqhd,bkhd->bhqk', qb2, k2).astype(jnp.float32) * scale, axis=-1)
        w = (p1 - lam * p2).astype(v.dtype)
        return jnp.einsum('bhqk,bkhd->bqhd', w, v)

    o = lax.map(one_block, (blocks(q1), blocks(q2)))
    o = o.transpose(1, 0, 2, 3, 4).reshape(b, n, DIFF_HEADS, DIFF_DV)
    o = rms_norm_2(o, subln_g) * (1.0 - lam_init)
    return o.reshape(b, n, GROUP_W)

def conformer_conv(a_val, a_gate, conv_w, conv_b, ln_g, ln_b):
    glu = a_val * jax.nn.sigmoid(a_gate)
    y = depthwise_conv(glu, conv_w) + conv_b
    return jax.nn.silu(layer_norm(y, ln_g, ln_b))

def spatial_gating(u, v, ln_g, ln_b, w_s, b_s):
    u = jax.nn.gelu(u)
    v = layer_norm(jax.nn.gelu(v), ln_g, ln_b)
    b, n, _ = v.shape
    vc = v.reshape(b, n // CHUNK, CHUNK, SG_GROUPS, SG_DIM)
    s = jnp.einsum('gpq,bcqgd->bcpgd', w_s, vc) + b_s.T[:, :, None]
    return u * s.reshape(b, n, GROUP_W)

def short_conv_mixer(bg, cg, xin, conv_w):
    return bg * depthwise_conv(cg * xin, conv_w)

def token_mixers(z, k1, k2, v, rope, lam, lam_init, conv_a_w, conv_a_b, ln_a_g, ln_a_b, subln_g,
                 sg_ln_g, sg_ln_b, sg_w, sg_b, conv_d_w, w_out):
    a_val, a_gate, q, _, _, u, sv, bg, cg, xin = z
    y_a = conformer_conv(a_val, a_gate, conv_a_w, conv_a_b, ln_a_g, ln_a_b)
    q1, q2 = qk_heads(q, rope)
    y_b = diff_attention(q1, q2, k1, k2, v, lam, lam_init, subln_g)
    y_c = spatial_gating(u, sv, sg_ln_g, sg_ln_b, sg_w, sg_b)
    y_d = short_conv_mixer(bg, cg, xin, conv_d_w)
    return jnp.concatenate([y_a, y_b, y_c, y_d], axis=-1) @ w_out

def channel_mixer(h, w1, w2):
    return jnp.square(jax.nn.relu(h @ w1)) @ w2

def second_inputs(seed: int = 0) -> dict:
    key = jax.random.key(seed)
    ks = jax.random.split(key, 32)

    def nrm(k, shape, scale):
        return jax.random.normal(k, shape, jnp.float32) * scale

    def gain(k, shape):
        return 1.0 + nrm(k, shape, 0.05)

    return {
        'x': nrm(ks[0], (BATCH, SEQ, D_MODEL), 1.0),
        'c': nrm(ks[1], (BATCH, D_MODEL), 1.0),
        'ctx': nrm(ks[2], (BATCH, CTX_LEN, D_MODEL), 1.0),
        'c_ctx': nrm(ks[3], (D_MODEL,), 1.0),
        'ada_w': nrm(ks[4], (DEPTH_2, D_MODEL, 6 * D_MODEL), 0.5 * D_MODEL ** -0.5),
        'ada_b': nrm(ks[5], (DEPTH_2, 6 * D_MODEL), 0.01),
        'norm1_g': gain(ks[6], (DEPTH_2, D_MODEL)),
        'norm2_g': gain(ks[7], (DEPTH_2, D_MODEL)),
        'w_in': nrm(ks[8], (DEPTH_2, D_MODEL, D_IN), D_MODEL ** -0.5),
        'conv_a_w': nrm(ks[9], (DEPTH_2, CONV_A_K, GROUP_W), CONV_A_K ** -0.5),
        'conv_a_b': nrm(ks[10], (DEPTH_2, GROUP_W), 0.01),
        'ln_a_g': gain(ks[11], (DEPTH_2, GROUP_W)),
        'ln_a_b': nrm(ks[12], (DEPTH_2, GROUP_W), 0.01),
        'lam_q1': nrm(ks[13], (DEPTH_2, DIFF_DQK), 0.1),
        'lam_k1': nrm(ks[14], (DEPTH_2, DIFF_DQK), 0.1),
        'lam_q2': nrm(ks[15], (DEPTH_2, DIFF_DQK), 0.1),
        'lam_k2': nrm(ks[16], (DEPTH_2, DIFF_DQK), 0.1),
        'subln_g': gain(ks[17], (DEPTH_2, DIFF_DV)),
        'sg_ln_g': gain(ks[18], (DEPTH_2, GROUP_W)),
        'sg_ln_b': nrm(ks[19], (DEPTH_2, GROUP_W), 0.01),
        'sg_w': nrm(ks[20], (DEPTH_2, SG_GROUPS, CHUNK, CHUNK), CHUNK ** -0.5),
        'sg_b': gain(ks[21], (DEPTH_2, SG_GROUPS, CHUNK)),
        'conv_d_w': nrm(ks[22], (DEPTH_2, CONV_D_K, GROUP_W), CONV_D_K ** -0.5),
        'w_out': nrm(ks[23], (DEPTH_2, D_MIX, D_MODEL), D_MIX ** -0.5),
        'mlp_w1': nrm(ks[24], (DEPTH_2, D_MODEL, D_FF), D_MODEL ** -0.5),
        'mlp_w2': nrm(ks[25], (DEPTH_2, D_FF, D_MODEL), D_FF ** -0.5),
        'final_g': gain(ks[26], (D_MODEL,)),
    }

def second_block(x, c, ctx, c_ctx, ada_w, ada_b, norm1_g, norm2_g, w_in, conv_a_w, conv_a_b, ln_a_g,
              ln_a_b, lam_q1, lam_k1, lam_q2, lam_k2, subln_g, sg_ln_g, sg_ln_b, sg_w, sg_b, conv_d_w,
              w_out, mlp_w1, mlp_w2, final_g):
    ROWS = x.shape[1] // GRID_W
    rope = axial_rope(ROWS, x.dtype)
    h_ctx = ctx
    for l in range(DEPTH_2):
        lam_init = 0.8 - 0.6 * math.exp(-0.3 * l)
        lam = (jnp.exp(jnp.sum(lam_q1[l] * lam_k1[l]).astype(jnp.float32))
               - jnp.exp(jnp.sum(lam_q2[l] * lam_k2[l]).astype(jnp.float32)) + lam_init)
        mod_x = jnp.split((jax.nn.silu(c) @ ada_w[l] + ada_b[l])[:, None, :], 6, axis=-1)
        mod_c = jnp.split(jax.nn.silu(c_ctx) @ ada_w[l] + ada_b[l], 6, axis=-1)
        mix_args = (rope, lam, lam_init, conv_a_w[l], conv_a_b[l], ln_a_g[l], ln_a_b[l], subln_g[l],
                    sg_ln_g[l], sg_ln_b[l], sg_w[l], sg_b[l], conv_d_w[l], w_out[l])

        hc = modulate(rms_norm_2(h_ctx, norm1_g[l]), mod_c[0], mod_c[1])
        zc = jnp.split(hc @ w_in[l], N_PARTS, axis=-1)
        k1c, k2c = qk_heads(zc[3], None)
        vc = v_heads(zc[4])

        hx = modulate(rms_norm_2(x, norm1_g[l]), mod_x[0], mod_x[1])
        zx = jnp.split(hx @ w_in[l], N_PARTS, axis=-1)
        k1x, k2x = qk_heads(zx[3], rope)
        k1 = jnp.concatenate([k1c, k1x], axis=1)
        k2 = jnp.concatenate([k2c, k2x], axis=1)
        v = jnp.concatenate([vc, v_heads(zx[4])], axis=1)
        x = x + mod_x[2] * token_mixers(zx, k1, k2, v, *mix_args)
        x = x + mod_x[5] * channel_mixer(modulate(rms_norm_2(x, norm2_g[l]), mod_x[3], mod_x[4]),
                                         mlp_w1[l], mlp_w2[l])

        if l < DEPTH_2 - 1:
            ctx_args = (None,) + mix_args[1:]
            h_ctx = h_ctx + mod_c[2] * token_mixers(zc, k1c, k2c, vc, *ctx_args)
            h_ctx = h_ctx + mod_c[5] * channel_mixer(
                modulate(rms_norm_2(h_ctx, norm2_g[l]), mod_c[3], mod_c[4]), mlp_w1[l], mlp_w2[l])
    return rms_norm_2(x, final_g)


def setup_inputs(seed=0):
    out = dict(first_inputs(seed))
    for name, value in second_inputs(seed + 1).items():
        if name != "x":
            out[name + "_2"] = value
    return out


def reference(
    x, c, w_mod, b_mod, g_pre, w_in, conv_w, conv_b, w_rg, b_rg, w_ig, b_ig, lru_lambda, w_pa,
    w_pb, w_o, g_post, c_2, ctx_2, c_ctx_2, ada_w_2, ada_b_2, norm1_g_2, norm2_g_2, w_in_2,
    conv_a_w_2, conv_a_b_2, ln_a_g_2, ln_a_b_2, lam_q1_2, lam_k1_2, lam_q2_2, lam_k2_2,
    subln_g_2, sg_ln_g_2, sg_ln_b_2, sg_w_2, sg_b_2, conv_d_w_2, w_out_2, mlp_w1_2, mlp_w2_2,
    final_g_2,
):
    x = first_block(
        x, c, w_mod, b_mod, g_pre, w_in, conv_w, conv_b, w_rg, b_rg, w_ig, b_ig, lru_lambda,
        w_pa, w_pb, w_o, g_post,
    )
    return second_block(
        x, c_2, ctx_2, c_ctx_2, ada_w_2, ada_b_2, norm1_g_2, norm2_g_2, w_in_2, conv_a_w_2,
        conv_a_b_2, ln_a_g_2, ln_a_b_2, lam_q1_2, lam_k1_2, lam_q2_2, lam_k2_2, subln_g_2,
        sg_ln_g_2, sg_ln_b_2, sg_w_2, sg_b_2, conv_d_w_2, w_out_2, mlp_w1_2, mlp_w2_2,
        final_g_2,
    )


_drawn_inputs = setup_inputs


def setup_inputs(seed=0):
    import zlib

    import numpy as np

    out = dict(_drawn_inputs(seed))
    spreads = {}
    factors = {'b_mod': 3.873,
     'g_pre': 3.011,
     'conv_b': 6.335,
     'b_rg': 60.387,
     'b_ig': 48.782,
     'g_post': 3.747,
     'conv_a_b_2': 8.0,
     'ln_a_g_2': 7.551,
     'ln_a_b_2': 64.0,
     'lam_q1_2': 4.619,
     'lam_k1_2': 6.512,
     'lam_q2_2': 8.0,
     'lam_k2_2': 8.0,
     'subln_g_2': 7.421,
     'sg_ln_g_2': 8.0,
     'sg_ln_b_2': 64.0,
     'sg_b_2': 7.877,
     'norm2_g_2': 4.059}
    for name, (base, spread) in spreads.items():
        noise = np.random.default_rng([zlib.crc32(name.encode()), seed]).standard_normal(out[name].shape)
        drawn = base * np.exp(spread * noise) if base else spread * noise
        out[name] = __import__('jax').numpy.asarray(drawn.astype(out[name].dtype))
    for name, factor in factors.items():
        out[name] = (out[name] * factor).astype(out[name].dtype)
    return out
```

```python
import math
from contextlib import ExitStack

import numpy as np

import concourse.bass as bass
from concourse import mybir

F32 = mybir.dt.float32
F32R = mybir.dt.float32r
ACT = mybir.ActivationFunctionType
ALU = mybir.AluOpType
AX_X = mybir.AxisListType.X

P = 128
D = 1024
KT = D // P
T = 512
TC = 256
DH = 128
EPS = 1e-6
TX = T + TC
NEG = -1e30
CW = 256
WF = KT * CW
MF = KT * P
L2 = 2
GW = 256
TAPS_A = 31
FF = 4096
NFB = FF // D
XPA = TX + 60
XPD = TX + 4
CONV_STEPS = 2 * TAPS_A
QSCALE = 32 ** -0.5
N_SMALL = 4 * 16

N_U, N_GL, N_MRG, N_PB, N_ATT, N_PA, N_WO = 4, 4, 8, 4, 10, 2, 4
C_U = 0
C_GL = C_U + N_U
C_MRG = C_GL + N_GL
C_PB = C_MRG + N_MRG
C_ATT = C_PB + N_PB
C_PA = C_ATT + 2 * N_ATT
C_WO = C_PA + N_PA
C_L = C_WO + N_WO
N_WIN, N_WOUT, N_FF = 10, 4, 8 * NFB
N_L = N_WIN + N_WOUT + N_FF
N_CHUNKS = C_L + L2 * N_L
M1, M2 = 24, 48
N_MV = M1 + L2 * M2
MV_RING = 3

VECS = [("c", 8), ("cc", 16), ("b_mod", 24), ("g_pre", 8), ("conv_w", 32), ("conv_b", 8),
        ("b_rg", 8), ("b_ig", 8), ("lru", 8), ("g_post", 8), ("final_g", 8)]
for _l in range(L2):
    VECS += [(f"ada_b{_l}", 96), (f"n1g{_l}", 16), (f"n2g{_l}", 16), (f"caw{_l}", 2 * TAPS_A),
             (f"cab{_l}", 2), (f"lag{_l}", 2), (f"lab{_l}", 2), (f"sgg{_l}", 2), (f"sgb{_l}", 2),
             (f"cdw{_l}", 6)]
VOFF, NV = {}, 0
for _n, _k in VECS:
    VOFF[_n] = (NV, _k)
    NV += _k


def ceil32(n):
    return (n + 31) // 32 * 32


class Map:

    def __init__(self, nc, base):
        self.nc, self.base = nc, ceil32(base)

    def at(self, name, shape, kb, dt=F32):
        n = 4
        for s in shape[1:]:
            n *= s
        assert self.base + int(kb * 1024) + n <= self.nc.sbuf_usable_end, name
        return self.nc.alloc_sbuf_tensor_at(name, list(shape), dt, offset=self.base + int(kb * 1024))



class Chain:

    def __init__(self, eng, sem):
        self.eng, self.sem, self.n, self.regs = eng, sem, 0, []

    def link(self, ins):
        ins.then_inc(self.sem, 1)
        self.n += 1
        value = self.n
        for reg, per in self.regs:
            value = reg * per + value
        self.eng.wait_ge(self.sem, value)

    def loop(self, count, per):
        return _ChainLoop(self, count, per)


class _ChainLoop:
    def __init__(self, chain, count, per):
        self.chain, self.count, self.per = chain, count, per

    def __enter__(self):
        self.start = self.chain.n
        self.fori = self.chain.eng.Fori(0, self.count)
        reg = self.fori.__enter__()
        self.chain.regs.append((reg, self.per))
        return reg

    def __exit__(self, *e):
        self.chain.regs.pop()
        self.fori.__exit__(*e)
        assert e[0] or self.chain.n - self.start == self.per, self.chain.n - self.start
        self.chain.n = self.start + self.per * self.count


class Norm:

    def __init__(self, all_, modulates, w=T):
        self.n, self.w = len(all_), w
        self.segs = 2 if w > T else 1
        self.sq = sum(KT * q.segs for q in all_)
        self.t = sum(KT * q.segs for q in all_ if q.mod)
        self.mod = modulates
        all_.append(self)


def tile(ap, i):
    return ap[:, bass.ds(i, 1), :].rearrange("p o t -> p (o t)")


def build(nc, wst, mst, vec, xin, cin, gst, cst, msk, rop, row, sgw, sgb, out):
    with ExitStack() as ctx:
        m = Map(nc, nc.sbuf_base)

        def sem(name):
            return ctx.enter_context(nc.semaphore(name))

        raw = [m.at(f"raw{s}", [P, WF], 8 * s) for s in range(2)]
        whi = [m.at(f"whi{s}", [P, WF], 16 + 8 * s, F32R) for s in range(2)]
        wlo = [m.at(f"wlo{s}", [P, WF], 32 + 8 * s, F32R) for s in range(2)]
        mvr = m.at("mvr", [P, MV_RING, KT, P], 48)
        xT = m.at("xT", [P, KT, T], 60)
        cT = m.at("cT", [P, KT, TC], 76)
        vecs = m.at("vecs", [P, NV], 84)
        consts = m.at("consts", [P, 4 * P], 86.5)
        ident, ones, perm = consts[:, 0:P], consts[:, P:2 * P], consts[:, 2 * P:3 * P]
        avg = consts[:, 3 * P:4 * P]
        small = m.at("small", [P, 512], 88.5)
        mask = m.at("mask", [P, 772], 90.5)
        hxh = m.at("hxh", [P, KT, T], 96, F32R)
        hxl = m.at("hxl", [P, KT, T], 112, F32R)

        def vcol(name, j=0, n=None):
            o, k = VOFF[name]
            return vecs[:, o + j:o + (k if n is None else j + n)]

        cols = [0]

        def scol(n):
            cols[0] += n
            return small[:, cols[0] - n:cols[0]]

        sc1, sc2 = scol(8), scol(16)
        mod1 = scol(24)
        a1, r1 = scol(8), scol(8)
        sp0 = cols[0]
        sp, nsp = scol(8), scol(8)
        l_abs, l_e, l_z, l_z2, l_q, l_m = (scol(8) for _ in range(6))
        varc, sdc, rsc = scol(8), scol(8), scol(8)
        nmx, lsum, rsum = scol(2), scol(2), scol(2)
        mod2_0 = cols[0]
        mod2 = scol(2 * M2)
        coef = [scol(16), scol(16)]
        scr = scol(64)
        lam_p, lam_x, lamc = scol(2), scol(2), scol(1)
        dnm, dls, drs = scol(4), scol(4), scol(4)
        oss, osd, ors = scol(24), scol(24), scol(24)

        acc = ctx.enter_context(nc.psum_tensor("acc", [P, 2, 1024], F32))
        aux = ctx.enter_context(nc.psum_tensor("aux", [P, 4, 512], F32))
        ps_mv = aux[:, 0, 0:96]
        ps_st = aux[:, 3, 0:8]
        bcast = aux[:, 1:3, :].rearrange("p a b -> p (a b)")

        gates = m.at("gates", [P, 2 * KT, T], 128)
        gate_a = gates[:, 0:KT, :]
        mix = gates[:, KT:2 * KT, :]
        uc = m.at("uc", [P, KT, T], 160)
        sg = m.at("sg", [P, KT, T], 176)
        bh = m.at("bh", [P, KT, T], 160, F32R)
        bl = m.at("bl", [P, KT, T], 176, F32R)
        lr = m.at("lr", [P, 7, T], 192)
        r_, i_, tau, a_, z_, x_, h_ = (lr[:, k, :] for k in range(7))
        wgate = m.at("wgate", [P, 2, 2 * P], 76)
        qkvg = m.at("qkvg", [P, 2 * N_ATT, T], 160)
        att = m.at("att", [P, 4, T], 76)
        vn = m.at("vn", [P, 12, P], 200)
        s_sb = m.at("s_sb", [P, 2, 768], 48)
        pt = m.at("pt", [P, 2, 768], 54)
        ath = m.at("ath", [P, 4, T], 160, F32R)
        atl = m.at("atl", [P, 4, T], 168, F32R)
        o32 = m.at("o32", [P, KT, T], 176)
        nsq = m.at("nsq", [P, KT, T], 160)
        nt_ = m.at("nt_", [P, 2, T], 192)
        nh_ = m.at("nh_", [P, 2, T], 196)
        ndg = m.at("ndg", [P, 4, P], 200)

        hch = m.at("hch", [P, KT, TC], 128, F32R)
        hcl = m.at("hcl", [P, KT, TC], 136, F32R)
        rope = m.at("rope", [P, 2, T], 90.5)
        rows = m.at("rows", [P, 192], 94.5)
        nsq2 = m.at("nsq2", [P, KT, T], 144)
        nsqc = m.at("nsqc", [P, KT, TC], 160)
        nt2 = m.at("nt2", [P, 2, TX], 168)
        nh2 = m.at("nh2", [P, 2, TX], 180)
        ndg2 = m.at("ndg2", [P, 6, P], 186)
        gpad = m.at("gpad", [P, 2, XPA], 144)
        aconv = m.at("aconv", [P, 2, XPA - 30], 150.5)
        qT = m.at("qT", [P, 2, TX], 156.75)
        kT = m.at("kT", [P, 2, TX], 162.75)
        vT = m.at("vT", [P, 2, TX], 168.75)
        vnat = m.at("vnat", [P, 6, GW], 174.75)
        av = m.at("av", [P, 2, TX], 174.75)
        ug = m.at("ug", [P, 2, TX], 180.75)
        svg = m.at("svg", [P, 2, TX], 186.75)
        bgt = m.at("bgt", [P, 2, TX], 192.75)
        cx = m.at("cx", [P, 2, XPD], 198.75)
        sigt = m.at("sigt", [P, 2, TX], 198.75)
        tmp = m.at("tmp", [P, TX], 204.8125)
        yca = m.at("yca", [P, 2, TX], 144)
        sqm = m.at("sqm", [P, 2, TX], 168.75)
        snat = m.at("snat", [P, 6, GW], 168.75)
        dconv = m.at("dconv", [P, 2, XPD - 2], 150.5)
        wsT = m.at("wsT", [P, 4, P], 48)
        bsg = m.at("bsg", [P, 2, P], 50)
        ndm = m.at("ndm", [P, 6, P], 51)
        prob = m.at("prob", [P, 2, 2, TX], 48)
        ptd = m.at("ptd", [P, 2, TX], 168.75)
        onat = m.at("onat", [P, 6, GW], 144)
        osq = m.at("osq", [P, 6, GW], 150.5)
        fxh = m.at("fxh", [P, KT, T], 144, F32R)
        fxl = m.at("fxl", [P, KT, T], 160, F32R)
        fch = m.at("fch", [P, KT, TC], 176, F32R)
        fcl = m.at("fcl", [P, KT, TC], 184, F32R)
        relu = m.at("relu", [P, 2, TX], 192)
        fsq = m.at("fsq", [P, 2, TX], 198)

        ld_small = sem("ld_small")
        w_loaded = [sem(f"w_loaded{s}") for s in range(2)]
        w_hi = sem("w_hi")
        w_lo = sem("w_lo")
        mv_loaded = [sem(f"mv_loaded{s}") for s in range(MV_RING)]
        mv_used = sem("mv_used")
        acc_ready = [sem(f"acc_ready{c}") for c in range(2)]
        acc_free = [sem(f"acc_free{c}") for c in range(2)]
        silu_c = sem("silu_c")
        mod_cols = sem("mod_cols")
        dve_step = sem("dve_step")
        n_sq, n_st, n_var, n_sd, n_dg, n_bc, n_t, n_h, n_out = (
            sem(f"norm_{x}") for x in ("sq", "st", "var", "sd", "dg", "bc", "t", "h", "out"))
        u_tap0 = sem("u_tap0")
        g_loaded = [sem(f"g_loaded{s}") for s in range(2)]
        lru_ps, lru_ri, lru_ta, lru_z, lru_sq, lru_out, lru_hi, lru_lo = (
            sem(f"lru_{x}") for x in ("ps", "ri", "ta", "z", "sq", "out", "hi", "lo"))
        lru_e, lru_sp = sem("lru_e"), sem("lru_sp")
        at_vt, at_vn, at_s, at_m, at_nm, at_e, at_p, at_t, at_pt, at_o, at_out = (
            sem(f"at_{x}") for x in ("vt", "vn", "s", "m", "nm", "e", "p", "t", "pt", "o", "out"))
        ath_done, atl_done = sem("ath_done"), sem("atl_done")
        pa_ready, pa_free = sem("pa_ready"), sem("pa_free")
        mix_done, mxh_done, mxl_done = sem("mix_done"), sem("mxh_done"), sem("mxl_done")
        x_done = sem("x_done")
        ld_ctx = sem("ld_ctx")
        ld_rope, ld_rows, ld_sg = sem("ld_rope"), sem("ld_rows"), sem("ld_sg")
        lam_s, lam_e, lam_ok = sem("lam_s"), sem("lam_e"), sem("lam_ok")
        glu, cx_zero, conv_step = sem("glu"), sem("cx_zero"), sem("conv_step")
        rot, roped = sem("rot"), sem("roped")
        v_t, v_nat = sem("v_t"), sem("v_nat")
        m_mean, m_cen, m_sq, m_st, m_var, m_sd, m_dg, m_bc, m_t, m_fin = (
            sem(f"ln_{x}") for x in ("mean", "cen", "sq", "st", "var", "sd", "dg", "bc", "t", "fin"))
        s_t, s_nat, s_mix, s_out, d_out = (sem(x) for x in ("sg_t", "sg_nat", "sg_mix", "sg_out", "d_out"))
        y_hi, y_lo = sem("y_hi"), sem("y_lo")
        q_s, q_m, q_e, q_w, q_t, q_pt, q_o, q_on = (
            sem(f"diff_{x}") for x in ("s", "m", "e", "w", "t", "pt", "o", "on"))
        o_sq, o_var, o_sd, o_n, o_t = (sem(f"sub_{x}") for x in ("sq", "var", "sd", "n", "t"))
        f_relu, f_hi, f_sq, f_lo = (sem(f"ff_{x}") for x in ("relu", "hi", "sq", "lo"))
        stored = sem("stored")

        norms = []
        n_pre = Norm(norms, True)
        n_post = Norm(norms, False)
        n_mix, n_ff = [], []
        for l in range(L2):
            n_mix.append(Norm(norms, True, TX))
            n_ff.append(Norm(norms, True, TX if l == 0 else T))
        n_fin = Norm(norms, False)
        assert [q.n for q in norms] == list(range(len(norms)))

        block = ctx.enter_context(nc.Block())

        def attend(pe, hp):
            base = 8 * hp
            for c in range(2):
                pe.wait_ge(acc_free[c], C_ATT + (hp + 1) * N_ATT)

            def scores(u):
                hh, r = (u // 4) % 2, u % 4
                if u >= base + 2:
                    pe.wait_ge(at_m, u - 1)
                for g in range(3):
                    q, k = qkvg[:, 2 * g + hh, r::4], qkvg[:, 6 + 2 * g + hh, :]
                    if g == 0:
                        pe.matmul(acc[:, u % 2, 0:T], q, k, start=True, stop=True)
                    else:
                        o = T + (g - 1) * P
                        last = pe.matmul(acc[:, u % 2, o:o + P], q, k[:, r::4], start=True, stop=True)
                last.then_inc(at_s, 1)

            def values(hh):
                head = 2 * hp + hh
                if head > 0:
                    pe.wait_ge(at_pt, 4 * head)
                    pe.wait_ge(at_out, 4 * head)
                for g in range(3):
                    v = qkvg[:, 12 + 2 * g + hh, :]
                    for r in range(4):
                        src = v[:, r * P:(r + 1) * P] if g == 0 else v[:, r::4]
                        last = pe.transpose(aux[:, 1 + g, r * P:(r + 1) * P], src, ident)
                    last.then_inc(at_vt, 1)

            for u in range(base, base + 8):
                hh, r = (u // 4) % 2, u % 4
                if u == base:
                    scores(u)
                if u + 1 < base + 8:
                    scores(u + 1)
                if r == 0:
                    values(hh)
                pe.wait_ge(at_p, u + 1)
                if r == 0:
                    pe.wait_ge(at_vn, 3 * (2 * hp + hh) + 3)
                else:
                    pe.wait_ge(at_pt, u)
                for b in range(6):
                    last = pe.transpose(aux[:, 1 + b // 4, (b % 4) * P:(b % 4 + 1) * P],
                                        s_sb[:, u % 2, b * P:(b + 1) * P], ident)
                last.then_inc(at_t, 1)
                pe.wait_ge(at_pt, u + 1)
                if hp == 0 and u == 1:
                    pe.wait_ge(mod_cols, 2)
                if r >= 2:
                    pe.wait_ge(at_out, u - 1)
                for b in range(6):
                    key = b if b < 4 else 4 * (b - 3) + r
                    last = pe.matmul(aux[:, 3 * (1 - u % 2), 0:P], vn[:, key, :],
                                     pt[:, u % 2, b * P:(b + 1) * P], start=(b == 0), stop=(b == 5))
                last.then_inc(at_o, 1)

        def attend_act(act, hp):
            base = 8 * hp
            for u in range(base - 1, base + 8):
                if u + 1 < base + 8:
                    act.wait_ge(at_nm, u + 2)
                    s = (u + 1) % 2
                    act.activation(s_sb[:, s, :], s_sb[:, s, :], ACT.Exp, bias=nmx[:, s:s + 1],
                                   accum_out=lsum[:, s:s + 1]).then_inc(at_e, 1)
                if u >= base:
                    act.wait_ge(at_t, u + 1)
                    if u >= 2:
                        act.wait_ge(at_o, u - 1)
                    act.activation(pt[:, u % 2, :].rearrange("p (a b) -> p a b", a=1),
                                   aux[:, 1:3, :].rearrange("p a b -> p (a b)")[:, 0:768].rearrange("p (a b) -> p a b", a=1),
                                   ACT.Copy).then_inc(at_pt, 1)
                if (u + 1) % 4 == 0 and u + 1 < base + 8:
                    head = (u + 1) // 4
                    if head > 0:
                        act.wait_ge(at_o, 4 * head)
                    for g in range(3):
                        act.wait_ge(at_vt, 3 * head + g + 1)
                        act.activation(vn[:, 4 * g:4 * g + 4, :], aux[:, 1 + g, :].rearrange("p (r d) -> p r d", d=P),
                                       ACT.Copy).then_inc(at_vn, 1)

        def attend_dve(dve, link, hp):
            base = 8 * hp
            for u in range(base - 1, base + 9):
                if u + 1 < base + 8:
                    v, s = u + 1, (u + 1) % 2
                    r = v % 4
                    dve.wait_ge(at_s, v + 1)
                    if v >= 2:
                        dve.wait_ge(at_t, v - 1)
                    dve.scalar_tensor_tensor(s_sb[:, s, 0:T], acc[:, s, 0:T], DH ** -0.5, mask[:, 3 - r:3 - r + T],
                                             ALU.mult, ALU.add)
                    dve.scalar_tensor_tensor(s_sb[:, s, T:768], acc[:, s, T:768], DH ** -0.5, mask[:, 516:772],
                                             ALU.mult, ALU.add).then_inc(at_m, 1)
                    dve.wait_ge(at_m, v + 1)
                    dve.tensor_reduce(nmx[:, s:s + 1], s_sb[:, s, :], AX_X, ALU.max, negate=True).then_inc(at_nm, 1)
                if base <= u < base + 8:
                    s = u % 2
                    dve.wait_ge(at_e, u + 1)
                    link(dve.reciprocal(rsum[:, s:s + 1], lsum[:, s:s + 1]))
                    dve.tensor_scalar(s_sb[:, s, :], s_sb[:, s, :], rsum[:, s:s + 1], None, ALU.mult
                                      ).then_inc(at_p, 1)
                if u - 1 >= base:
                    v = u - 1
                    hh, r = (v // 4) % 2, v % 4
                    dve.wait_ge(at_o, v + 1)
                    dve.tensor_tensor(att[:, 2 * hp + hh, r::4], aux[:, 3 * (1 - v % 2), 0:P],
                                      qkvg[:, 2 * (N_ATT - 1) + hh, r::4], ALU.mult).then_inc(at_out, 1)

        def layer(pe, l, gemm, matvec, norm_sums):
            X, XC = [(hxh, hxl, 0, T)], [(hxh, hxl, 0, T), (hch, hcl, T, TC)]
            base = C_L + l * N_L
            own = XC if l == 0 else X
            nj = 6 if l == 0 else 4
            norm_sums(n_mix[l], [(nsq2, T), (nsqc, TC)], ndg2)
            pe.wait_ge(n_out, n_mix[l].t + 2 * KT)
            if l == 0:
                with pe.Fori(0, N_WIN // 2) as i:
                    for s in range(2):
                        gemm(2 * i + s + base, s, XC)
            else:
                for j in range(6):
                    gemm(base + j, j % 2, XC if j in (3, 4) else X)
                with pe.Fori(3, N_WIN // 2) as i:
                    for s in range(2):
                        gemm(2 * i + s + base, s, X)
            for c in range(2):
                pe.wait_ge(acc_free[c], base + N_WIN)
            for b, src in enumerate((qT, kT)):
                for c in range(2):
                    last = pe.matmul(aux[:, 2 * b + c, :], perm, src[:, c, 0:T], start=True, stop=True)
            last.then_inc(rot, 1)
            flat = acc[:].rearrange("p a b -> p (a b)")
            for j in range(6):
                for c in range(2):
                    last = pe.transpose(flat[:, j * GW + c * P:j * GW + (c + 1) * P],
                                        vT[:, c, j * P:(j + 1) * P], ident)
            last.then_inc(v_t, 1)

            def ln(q, src, cuts):
                for c in range(2):
                    for o, so, w in cuts:
                        last = pe.matmul(acc[:, 0, o:o + w], avg, src[:, c, so:so + w], start=(c == 0), stop=(c == 1),
                                         skip_group_check=True)
                last.then_inc(m_mean, 1)
                pe.wait_ge(m_sq, 2 * q + 2)
                for j in range(nj):
                    for c in range(2):
                        last = pe.matmul(ps_st[:, j:j + 1], sqm[:, c, j * P:(j + 1) * P], ones[:, 0:1],
                                         start=(c == 0), stop=(c == 1))
                last.then_inc(m_st, 1)
                pe.wait_ge(m_dg, q + 1)
                for j in range(nj):
                    last = pe.matmul(bcast[:, j * P:(j + 1) * P], ones, ndm[:, j, :], start=True, stop=True)
                last.then_inc(m_bc, 1)

            pe.wait_ge(roped, 4 * l + 4)
            pe.wait_ge(v_nat, 3 * l + 3)
            pe.wait_ge(conv_step, CONV_STEPS * (l + 1))
            ln(2 * l, aconv, [(0, 0, T), (T, T + 30, TC)] if l == 0 else [(0, 0, T)])
            ln(2 * l + 1, svg, [(0, 0, T), (T, T, TC)] if l == 0 else [(0, 0, T)])
            pe.wait_ge(m_fin, 4 * l + 4)
            for j in range(nj):
                for c in range(2):
                    last = pe.transpose(flat[:, j * GW + c * P:j * GW + (c + 1) * P],
                                        svg[:, c, j * P:(j + 1) * P], ident)
            last.then_inc(s_t, 1)
            pe.wait_ge(s_nat, (nj // 2) + 3 * l)
            pe.wait_ge(ld_sg, 32 * (l + 1))
            for g in range(4):
                half = 64 * (g % 2)
                for j in range(nj):
                    last = pe.matmul(acc[half:half + 64, g // 2, j * P:(j + 1) * P],
                                     snat[:, j, 64 * g:64 * g + 64], wsT[:, g, :], start=True, stop=True)
            last.then_inc(s_mix, 1)
            pe.wait_ge(s_out, 2 * l + 2)
            units = [(h, j) for h in range(4) for j in range(nj)]
            u0 = 24 * l

            def scores(u):
                h, j = units[u]
                for i in range(2):
                    if u > 0:
                        pe.wait_ge(q_e, 2 * (u0 + u - 1) + i + 1)
                    f = 64 * (h % 2) + 32 * i
                    q = qT[f:f + 32, h // 2, j * P:(j + 1) * P]
                    for o, w in ((0, T), (T, TC)) if j < 4 else ((T, TC),):
                        last = pe.matmul(acc[:, i, o:o + w], q, kT[f:f + 32, h // 2, o:o + w], start=True, stop=True)
                    last.then_inc(q_s, 1)

            scores(0)
            for u, (h, j) in enumerate(units):
                if u + 1 < len(units):
                    scores(u + 1)
                first = 0 if j < 4 else 4
                pe.wait_ge(q_w, u0 + u + 1)
                if u > 0:
                    pe.wait_ge(q_pt, u0 + u)
                for b in range(first, 6):
                    last = pe.transpose(bcast[:, b * P:(b + 1) * P], prob[:, u % 2, 0, b * P:(b + 1) * P], ident)
                last.then_inc(q_t, 1)
                pe.wait_ge(q_pt, u0 + u + 1)
                if u >= 2:
                    pe.wait_ge(q_on, u0 + u - 1)
                for b in range(first, 6):
                    last = pe.matmul(aux[:, 3 * (1 - u % 2), 0:64], ptd[:, u % 2, b * P:(b + 1) * P],
                                     vnat[:, b, 64 * h:64 * h + 64], start=(b == first), stop=(b == 5))
                last.then_inc(q_o, 1)
            pe.wait_ge(o_n, l + 1)
            for j in range(nj):
                for c in range(2):
                    last = pe.transpose(acc[:, c, j * P:(j + 1) * P], onat[:, j, c * P:(c + 1) * P], ident)
            last.then_inc(o_t, 1)
            pe.wait_ge(y_lo, KT * (l + 1))
            base += N_WIN
            with pe.Fori(0, N_WOUT // 2) as i:
                for s in range(2):
                    gemm(2 * i + s + base, s, own)
            norm_sums(n_ff[l], [(nsq2, T), (nsqc, TC)] if l == 0 else [(nsq2, T)], ndg2)
            pe.wait_ge(n_out, n_ff[l].t + KT * len(own))
            base += N_WOUT
            hid = [(fxh, fxl, 0, T), (fch, fcl, T, TC)] if l == 0 else [(fxh, fxl, 0, T)]
            with pe.Fori(0, NFB) as b:
                for kind in range(2):
                    for i in range(2):
                        for s in range(2):
                            n = 8 * b + (base + 4 * kind + 2 * i + s)
                            if kind == 1 and i == 0 and s == 0:
                                pe.wait_ge(f_lo, KT * b + (KT * NFB * l + KT))
                            gemm(n, s, hid if kind else own)
                        if l == 0:
                            for v in range(MV_RING):
                                q = MV_RING * (2 * kind + i) + v
                                matvec(v, 64 * b + 16 * ((M1 + M2 + q) // MV_RING + 1),
                                       tile(ps_mv.rearrange("p (a b) -> p a b", b=2), 12 * b + q),
                                       lambda k: sc2[:, 2 * k:2 * k + 2])

        def layer_act(act, l, split, norm_squares, norm_root, norm_modulate2):
            base = C_L + l * N_L
            two = l == 0
            wx = TX if two else T
            nj = wx // P
            if l == 0:
                for k in range(KT):
                    act.wait_ge(x_done, k + 1)
                    act.activation(nsq2[:, k, :], xT[:, k, :], ACT.Square).then_inc(n_sq, 1)
                act.wait_ge(ld_ctx, 16)
                norm_squares(cT, nsqc)
            else:
                act.wait_ge(acc_ready[1], base)
                for k in range(KT):
                    act.wait_ge(acc_free[k % 2], base - 4 + k // 2 + 1)
                    act.activation(nsq2[:, k, :], xT[:, k, :], ACT.Square).then_inc(n_sq, 1)
                    act.activation(nsqc[:, k, :], cT[:, k, :], ACT.Square).then_inc(n_sq, 1)
            act.wait_ge(lam_s, l + 1)
            act.activation(lam_x, lam_p, ACT.Exp).then_inc(lam_e, 1)
            norm_root(n_mix[l])
            act.wait_ge(mod_cols, l + 3)
            norm_modulate2(n_mix[l], l, 0, [(hxh, 0, T, 0), (hch, T, TC, 1)])
            kinds = [(av, ACT.Copy), (sigt, ACT.Sigmoid), (qT, ACT.Copy), (kT, ACT.Copy), (vT, ACT.Copy),
                     (ug, ACT.Gelu_apprx_tanh), (svg, ACT.Gelu_apprx_tanh), (bgt, ACT.Copy), (cx, ACT.Copy)]
            for j, (dst, func) in enumerate(kinds):
                n = base + j
                wj = TX if two or j in (3, 4) else T
                if j == 4:
                    act.wait_ge(glu, 2 * l + 2)
                if j == 8:
                    act.wait_ge(cx_zero, l + 1)
                for c in range(2):
                    act.wait_ge(acc_ready[c], n + 1)
                    if j == 8:
                        for o, d, w in ((0, 1, T), (T, T + 3, TC))[:2 if two else 1]:
                            ins = act.activation(cx[:, c, d:d + w], acc[:, c, o:o + w], func)
                    elif j == 2 and two:
                        act.activation(dst[:, c, 0:T], acc[:, c, 0:T], func)
                        ins = act.activation(dst[:, c, T:TX], acc[:, c, T:TX], func, scale=QSCALE)
                    else:
                        ins = act.activation(dst[:, c, 0:wj], acc[:, c, 0:wj], func)
                    ins.then_inc(acc_free[c], 1)
                split(n + 2, n % 2, n // 2 + 1)
            n = base + N_WIN - 1
            split(n + 2, n % 2, n // 2 + 1)
            flat = acc[:].rearrange("p a b -> p (a b)")
            act.wait_ge(v_t, l + 1)
            for j in range(3):
                act.activation(vnat[:, 2 * j:2 * j + 2, :].rearrange("p a b -> p (a b)"),
                               flat[:, 512 * j:512 * j + 512], ACT.Copy).then_inc(v_nat, 1)

            def y_split(src, c, k, y):
                act.activation(hxh[:, k, :], src[:, c, 0:T], ACT.Copy).then_inc(y_hi, 1)
                if two:
                    act.activation(hch[:, k, :], src[:, c, T:TX], ACT.Copy).then_inc(y_hi, 1)

            def ln(q, src, func, g, b):
                for c in range(2):
                    act.wait_ge(m_cen, 2 * q + c + 1)
                    act.activation(sqm[:, c, 0:wx], src[:, c, 0:wx], ACT.Square).then_inc(m_sq, 1)
                act.wait_ge(m_var, q + 1)
                act.activation(sdc[:, 0:nj], varc[:, 0:nj], ACT.Sqrt).then_inc(m_sd, 1)
                for c in range(2):
                    act.wait_ge(m_t, 2 * q + c + 1)
                    act.activation(src[:, c, 0:wx], src[:, c, 0:wx], func, bias=vcol(b, c, 1),
                                   scale=vcol(g, c, 1)).then_inc(m_fin, 1)

            ln(2 * l, yca, ACT.Silu, f"lag{l}", f"lab{l}")
            act.wait_ge(m_fin, 4 * l + 2)
            for c in range(2):
                y_split(yca, c, c, c)
            ln(2 * l + 1, svg, ACT.Identity, f"sgg{l}", f"sgb{l}")
            act.wait_ge(s_t, l + 1)
            for j in range(nj // 2):
                act.activation(snat[:, 2 * j:2 * j + 2, :].rearrange("p a b -> p (a b)"),
                               flat[:, 512 * j:512 * j + 512], ACT.Copy).then_inc(s_nat, 1)
            for c in range(2):
                act.wait_ge(s_out, 2 * l + c + 1)
                y_split(ug, c, 4 + c, 2 + c)
            for c in range(2):
                act.wait_ge(d_out, 2 * l + c + 1)
                y_split(bgt, c, 6 + c, 4 + c)
            units = [(h, j) for h in range(4) for j in range(nj)]
            u0 = 24 * l

            def exps(u):
                o = 0 if units[u][1] < 4 else T
                if u == 0:
                    act.wait_ge(s_mix, l + 1)
                    act.wait_ge(m_bc, 2 * l + 2)
                    act.wait_ge(s_out, 2 * l + 2)
                if u >= 2:
                    act.wait_ge(q_t, u0 + u - 1)
                for i in range(2):
                    act.wait_ge(q_m, 2 * (u0 + u) + i + 1)
                    z = 2 * (u % 2) + i
                    act.activation(prob[:, u % 2, i, o:TX], acc[:, i, o:TX], ACT.Exp, bias=dnm[:, z:z + 1],
                                   accum_out=dls[:, z:z + 1]).then_inc(q_e, 1)

            def out(u):
                h, j = units[u]
                act.wait_ge(q_o, u0 + u + 1)
                act.activation(onat[:, j, 64 * h:64 * h + 64], aux[:, 3 * (1 - u % 2), 0:64], ACT.Copy
                               ).then_inc(q_on, 1)

            exps(0)
            for u, (h, j) in enumerate(units):
                if u + 1 < len(units):
                    exps(u + 1)
                if u > 0:
                    out(u - 1)
                o = 0 if j < 4 else T
                act.wait_ge(q_t, u0 + u + 1)
                act.activation(ptd[:, u % 2, o:TX], bcast[:, o:TX], ACT.Copy).then_inc(q_pt, 1)
            out(len(units) - 1)
            act.wait_ge(q_on, u0 + len(units))
            act.activation(osq[:, 0:nj, :], onat[:, 0:nj, :], ACT.Square).then_inc(o_sq, 1)
            act.wait_ge(o_var, l + 1)
            act.activation(osd[:, 0:4 * nj], oss[:, 0:4 * nj], ACT.Sqrt).then_inc(o_sd, 1)
            act.wait_ge(o_t, l + 1)
            for c in range(2):
                y_split(acc, c, 2 + c, 6 + c)
            base += N_WIN
            with act.Fori(0, N_WOUT // 2) as i:
                for s in range(2):
                    n = 2 * i + s + base
                    for c in range(2):
                        act.wait_ge(acc_free[c], n + 1)
                        act.activation(tile(nsq2, 4 * i + 2 * s + c), tile(xT, 4 * i + 2 * s + c), ACT.Square
                                       ).then_inc(n_sq, 1)
                        if two:
                            act.activation(tile(nsqc, 4 * i + 2 * s + c), tile(cT, 4 * i + 2 * s + c), ACT.Square
                                           ).then_inc(n_sq, 1)
                    split(n + 2, s, i + base // 2 + 1)
            norm_root(n_ff[l])
            norm_modulate2(n_ff[l], l, 1, [(hxh, 0, T, 0), (hch, T, TC, 1)][:2 if two else 1])
            base += N_WOUT

            def ff(b, end=False):
                for i in range(2):
                    for s in range(2):
                        n = 8 * b + (base + 2 * i + s)
                        for c in range(2):
                            t = 4 * i + 2 * s + c
                            f0 = KT * b + (KT * NFB * l + t)
                            act.wait_ge(acc_ready[c], n + 1)
                            act.wait_ge(f_sq, f0 + 1)
                            act.activation(relu[:, c, 0:wx], acc[:, c, 0:wx], ACT.Relu).then_inc(acc_free[c], 1)
                            act.wait_ge(acc_free[c], n + 1)
                            ins = act.activation(fxh[:, t, :], relu[:, c, 0:T], ACT.Square)
                            if two:
                                ins = act.activation(fch[:, t, :], relu[:, c, T:TX], ACT.Square)
                            ins.then_inc(f_hi, 1)
                        split(n + 2, s, 4 * b + (base // 2 + i + 1))
                for i in range(1 if end else 2):
                    for s in range(2):
                        split(8 * b + (base + 4 + 2 * i + s + 2), s, 4 * b + (base // 2 + 2 + i + 1))

            with act.Fori(0, NFB - l) as b:
                ff(b)
            if l == L2 - 1:
                ff(NFB - 1, end=True)

        def layer_dve(dve, link, l, split, norm_scale, norm_modulate2, chain):
            base = C_L + l * N_L
            two = l == 0
            wx = TX if two else T
            nj = wx // P
            lam_init = 0.8 - 0.6 * math.exp(-0.3 * l)
            dve.wait_ge(ld_rows, 16 * (l + 1))
            for i in range(2):
                link(dve.tensor_tensor(scr[:, 32 * i:32 * i + 32], rows[:, 64 + 64 * i:96 + 64 * i],
                                       rows[:, 96 + 64 * i:128 + 64 * i], ALU.mult))
            dve.tensor_reduce(lam_p, scr.rearrange("p (i d) -> p i d", i=2), AX_X, ALU.add).then_inc(lam_s, 1)
            for i, g in enumerate(("n1g", "n2g")):
                o = 2 * KT * (3 * i + 1)
                ins = dve.scalar_tensor_tensor(coef[i], mod2[:, o:o + 2 * KT], 1.0, vcol(f"{g}{l}"), ALU.add, ALU.mult)
            ins.then_inc(mod_cols, 1)
            dve.wait_ge(lam_e, l + 1)
            link(dve.scalar_tensor_tensor(lamc, lam_x[:, 0:1], lam_init, lam_x[:, 1:2], ALU.add, ALU.subtract))
            norm_scale(n_mix[l], ndg2)
            norm_modulate2(n_mix[l], [(xT, hxh, hxl, 0, T), (cT, hch, hcl, T, TC)])
            dve.memset(gpad[:], 0.0)
            wc = XPA - 30 if two else T
            segs = [(0, 15, T), (T, T + 45, TC)][:2 if two else 1]
            step = 0
            for j in range(N_WIN):
                n = base + j
                if j == 1:
                    link(dve.memset(sc1, 0.0))
                    for c in range(2):
                        dve.wait_ge(acc_free[c], n + 1)
                        for o, d, w in segs:
                            ins = dve.tensor_tensor(gpad[:, c, d:d + w], av[:, c, o:o + w], sigt[:, c, o:o + w], ALU.mult)
                        ins.then_inc(glu, 1)
                    dve.wait_ge(glu, 2 * l + 2)
                    dve.memset(cx[:], 0.0).then_inc(cx_zero, 1)
                if j == N_WIN - 1:
                    for c in range(2):
                        dve.wait_ge(acc_ready[c], n + 1)
                        for o, d, w in [(0, 1, T), (T, T + 3, TC)][:2 if two else 1]:
                            if c == 0 and o == 0:
                                dve.wait_ge(acc_free[1], n)
                            ins = dve.tensor_tensor(cx[:, c, d:d + w], acc[:, c, o:o + w], cx[:, c, d:d + w], ALU.mult)
                        ins.then_inc(acc_free[c], 1)
                if j >= 2:
                    for _ in range(min(8, CONV_STEPS - step)):
                        tap, c = step // 2, step % 2
                        w = vcol(f"caw{l}", c * TAPS_A + tap, 1)
                        if tap == 0:
                            ins = dve.tensor_scalar(aconv[:, c, 0:wc], gpad[:, c, 0:wc], w, vcol(f"cab{l}", c, 1),
                                                    ALU.mult, ALU.add)
                        else:
                            dve.wait_ge(conv_step, CONV_STEPS * l + step - 1)
                            ins = dve.scalar_tensor_tensor(aconv[:, c, 0:wc], gpad[:, c, tap:tap + wc], w,
                                                           aconv[:, c, 0:wc], ALU.mult, ALU.add)
                        ins.then_inc(conv_step, 1)
                        step += 1
                split(n + 2, n % 2)
            assert step == CONV_STEPS
            dve.wait_ge(rot, l + 1)
            for b, (src, scale) in enumerate(((qT, QSCALE), (kT, 1.0))):
                for c in range(2):
                    if b or c:
                        dve.wait_ge(roped, 4 * l + 2 * b + c)
                    dve.scalar_tensor_tensor(tmp[:, 0:T], aux[:, 2 * b + c, :], scale, rope[:, 1, :], ALU.mult, ALU.mult)
                    link(dve.scalar_tensor_tensor(src[:, c, 0:T], src[:, c, 0:T], scale, rope[:, 0, :],
                                                  ALU.mult, ALU.mult))
                    dve.tensor_tensor(src[:, c, 0:T], src[:, c, 0:T], tmp[:, 0:T], ALU.add).then_inc(roped, 1)

            def y_split(src, c, k, y):
                per = 2 if two else 1
                dve.wait_ge(y_hi, 2 * KT * l + per * (y + 1))
                ins = dve.tensor_tensor(hxl[:, k, :], src[:, c, 0:T], hxh[:, k, :].bitcast(F32), ALU.subtract)
                if two:
                    ins = dve.tensor_tensor(hcl[:, k, :], src[:, c, T:TX], hch[:, k, :].bitcast(F32), ALU.subtract)
                ins.then_inc(y_lo, 1)

            def ln(q, src, dst, cuts):
                dve.wait_ge(m_mean, q + 1)
                for c in range(2):
                    for o, so, w in cuts:
                        ins = dve.tensor_tensor(dst[:, c, o:o + w], src[:, c, so:so + w], acc[:, 0, o:o + w],
                                                ALU.subtract)
                    ins.then_inc(m_cen, 1)
                dve.wait_ge(m_st, q + 1)
                dve.tensor_scalar(varc[:, 0:nj], ps_st[:, 0:nj], 1.0 / GW, EPS, ALU.mult, ALU.add).then_inc(m_var, 1)
                dve.wait_ge(m_sd, q + 1)
                link(dve.reciprocal(rsc[:, 0:nj], sdc[:, 0:nj]))
                for j in range(nj):
                    ins = dve.tensor_scalar(ndm[:, j, :], ident, rsc[:, j:j + 1], None, ALU.mult)
                ins.then_inc(m_dg, 1)
                dve.wait_ge(m_bc, q + 1)
                for c in range(2):
                    dve.tensor_tensor(dst[:, c, 0:wx], dst[:, c, 0:wx], bcast[:, 0:wx], ALU.mult).then_inc(m_t, 1)

            ln(2 * l, aconv, yca, [(0, 0, T), (T, T + 30, TC)] if two else [(0, 0, T)])
            for c in range(2):
                y_split(yca, c, c, c)
            ln(2 * l + 1, svg, svg, [(0, 0, wx)])
            dve.wait_ge(s_mix, l + 1)
            for c in range(2):
                if c:
                    dve.wait_ge(s_out, 2 * l + 1)
                link(dve.tensor_tensor(tmp[:, 0:wx].rearrange("p (j q) -> p j q", q=P),
                                       acc[:, c, 0:wx].rearrange("p (j q) -> p j q", q=P),
                                       bsg[:, c:c + 1, :].to_broadcast([P, nj, P]), ALU.add))
                dve.tensor_tensor(ug[:, c, 0:wx], tmp[:, 0:wx], ug[:, c, 0:wx], ALU.mult).then_inc(s_out, 1)
            for c in range(2):
                y_split(ug, c, 4 + c, 2 + c)
            wd = XPD - 2 if two else T
            for c in range(2):
                w = [vcol(f"cdw{l}", 3 * c + tap, 1) for tap in range(3)]
                link(dve.tensor_scalar(dconv[:, c, 0:wd], cx[:, c, 0:wd], w[0], None, ALU.mult))
                for tap in range(1, 3):
                    link(dve.scalar_tensor_tensor(dconv[:, c, 0:wd], cx[:, c, tap:tap + wd], w[tap],
                                                  dconv[:, c, 0:wd], ALU.mult, ALU.add))
                for o, d, w_ in [(0, 0, T), (T, T + 2, TC)][:2 if two else 1]:
                    ins = dve.tensor_tensor(bgt[:, c, o:o + w_], dconv[:, c, d:d + w_], bgt[:, c, o:o + w_], ALU.mult)
                ins.then_inc(d_out, 1)
            for c in range(2):
                y_split(bgt, c, 6 + c, 4 + c)
            units = [(h, j) for h in range(4) for j in range(nj)]
            u0 = 24 * l

            def maxima(u):
                o = 0 if units[u][1] < 4 else T
                for i in range(2):
                    z = 2 * (u % 2) + i
                    dve.wait_ge(q_s, 2 * (u0 + u) + i + 1)
                    dve.tensor_reduce(dnm[:, z:z + 1], acc[:, i, o:TX], AX_X, ALU.max, negate=True).then_inc(q_m, 1)

            maxima(0)
            for u, (h, j) in enumerate(units):
                if u + 1 < len(units):
                    maxima(u + 1)
                o = 0 if j < 4 else T
                z = 2 * (u % 2)
                dve.wait_ge(q_e, 2 * (u0 + u) + 2)
                link(dve.reciprocal(drs[:, z:z + 2], dls[:, z:z + 2]))
                link(dve.tensor_tensor(drs[:, z + 1:z + 2], drs[:, z + 1:z + 2], lamc, ALU.mult))
                p1, p2 = prob[:, u % 2, 0, o:TX], prob[:, u % 2, 1, o:TX]
                link(dve.tensor_scalar(p2, p2, drs[:, z + 1:z + 2], None, ALU.mult))
                dve.scalar_tensor_tensor(p1, p1, drs[:, z:z + 1], p2, ALU.mult, ALU.subtract).then_inc(q_w, 1)
            ng = 4 * nj
            dve.wait_ge(o_sq, l + 1)
            link(dve.tensor_reduce(oss[:, 0:ng], osq[:, 0:nj, :].rearrange("p j (h d) -> p (j h) d", h=4), AX_X, ALU.add))
            dve.tensor_scalar(oss[:, 0:ng], oss[:, 0:ng], 1.0 / 64, EPS, ALU.mult, ALU.add).then_inc(o_var, 1)
            dve.wait_ge(o_sd, l + 1)
            link(dve.reciprocal(ors[:, 0:ng], osd[:, 0:ng]))
            o3 = onat[:, 0:nj, :].rearrange("p j (h d) -> p (j h) d", h=4)
            link(dve.tensor_tensor(o3, o3, ors[:, 0:ng].rearrange("p (g o) -> p g o", o=1).to_broadcast([P, ng, 64]),
                                   ALU.mult))
            dve.scalar_tensor_tensor(o3, o3, 1.0 - lam_init,
                                     rows[:, 0:64].rearrange("p (o d) -> p o d", o=1).to_broadcast([P, ng, 64]),
                                     ALU.mult, ALU.mult).then_inc(o_n, 1)
            for c in range(2):
                y_split(acc, c, 2 + c, 6 + c)

            def residual(t, c, part):
                for dst, o, w, z in ((xT, 0, T, 0), (cT, T, TC, 1))[:2 if two else 1]:
                    g0 = mod2_0 + 2 * (3 * KT * part + 2 * KT) + z
                    x_ = tile(dst, t)
                    ins = dve.scalar_tensor_tensor(x_, acc[:, c, o:o + w], small[:, bass.ds(2 * t + g0, 1)], x_,
                                                   ALU.mult, ALU.add)
                ins.then_inc(acc_free[c], 1)

            base += N_WIN
            with dve.Fori(0, N_WOUT // 2) as i:
                for s in range(2):
                    n = 2 * i + s + base
                    for c in range(2):
                        dve.wait_ge(acc_ready[c], n + 1)
                        residual(4 * i + (2 * s + c), c, 0)
                    split(n + 2, s)
            norm_scale(n_ff[l], ndg2)
            norm_modulate2(n_ff[l], [(xT, hxh, hxl, 0, T), (cT, hch, hcl, T, TC)][:2 if two else 1])
            base += N_WOUT

            def ff(b, end=False):
                for i in range(2):
                    for s in range(2):
                        n = 8 * b + (base + 2 * i + s)
                        for c in range(2):
                            t = 4 * i + 2 * s + c
                            f0 = KT * b + (KT * NFB * l + t)
                            dve.wait_ge(acc_free[c], n + 1)
                            dve.tensor_tensor(fsq[:, c, 0:wx], relu[:, c, 0:wx], relu[:, c, 0:wx], ALU.mult
                                              ).then_inc(f_sq, 1)
                            dve.wait_ge(f_sq, f0 + 3)
                            dve.wait_ge(f_hi, f0 + 1)
                            ins = dve.tensor_tensor(fxl[:, t, :], fsq[:, c, 0:T], fxh[:, t, :].bitcast(F32), ALU.subtract)
                            if two:
                                ins = dve.tensor_tensor(fcl[:, t, :], fsq[:, c, T:TX], fch[:, t, :].bitcast(F32),
                                                        ALU.subtract)
                            ins.then_inc(f_lo, 1)
                        split(n + 2, s)
                for i in range(2):
                    for s in range(2):
                        n = 8 * b + (base + 4 + 2 * i + s)
                        for c in range(2):
                            dve.wait_ge(acc_ready[c], n + 1)
                            residual(4 * i + 2 * s + c, c, 1)
                        if not (end and i == 1):
                            split(n + 2, s)

            with dve.Fori(0, NFB - l) as b:
                ff(b)
            if l == L2 - 1:
                ff(NFB - 1, end=True)
            else:
                dve.wait_ge(mv_used, N_MV)
                for c in range(2):
                    dve.wait_ge(acc_free[c], C_L + N_L)
                link(dve.tensor_tensor(mod2, ps_mv, vcol("ada_b1"), ALU.add))

        @block.sync
        def _(sync):
            def load_mv(n, s):
                if isinstance(n, int) and n < MV_RING:
                    pass
                else:
                    sync.wait_ge(mv_used, n - MV_RING + 1)
                sync.dma_start(mvr[:, s, :, :], mst[bass.ds(n, 1)].rearrange("o p (k f) -> (o p) k f", k=KT)
                               ).then_inc(mv_loaded[s], 16)

            def load_w(n, s):
                sync.wait_ge(w_lo, n - 1)
                sync.dma_start(raw[s][:], wst[bass.ds(n, 1)].rearrange("o p f -> (o p) f")
                               ).then_inc(w_loaded[s], 16)

            for n in range(MV_RING):
                load_mv(n, n)
            for s in range(2):
                sync.dma_start(raw[s][:], wst[s]).then_inc(w_loaded[s], 16)
            with sync.Fori(1, M1 // MV_RING) as i:
                for s in range(MV_RING):
                    load_mv(MV_RING * i + s, s)
            with sync.Fori(1, C_MRG // 2 + 1) as i:
                for s in range(2):
                    load_w(2 * i + s, s)
            with sync.Fori(0, N_MRG // 2) as i:
                for s in range(2):
                    load_w(2 * i + s + C_MRG + 2, s)
                    for b in range(2 * MV_RING):
                        load_mv(12 * i + (M1 + 6 * s + b), b % MV_RING)
            with sync.Fori((C_MRG + N_MRG) // 2 + 1, (C_L + N_WIN + N_WOUT) // 2 + 1) as i:
                for s in range(2):
                    load_w(2 * i + s, s)
            sync.wait_ge(y_lo, KT)
            with sync.Fori(0, N_FF // 2) as i:
                for s in range(2):
                    load_w(2 * i + s + (C_L + N_WIN + N_WOUT + 2), s)
                for b in range(MV_RING):
                    load_mv(MV_RING * i + (M1 + M2 + b), b)
            with sync.Fori((C_L + N_L) // 2 + 1, N_CHUNKS // 2) as i:
                for s in range(2):
                    load_w(2 * i + s, s)
            sync.wait_ge(x_done, 2 * KT)
            sync.dma_start(out, xT[:]).then_inc(stored, 16)
            sync.wait_ge(stored, 16)

        @block.gpsimd
        def _(pool):
            for j in range(KT):
                if j >= 2:
                    pool.wait_ge(lru_ps, j - 1)
                pool.dma_start(wgate[:, j % 2, :], gst[j]).then_inc(g_loaded[j % 2], 16)
            pool.wait_ge(at_out, 16)
            pool.dma_start(rope[:], rop).then_inc(ld_rope, 16)
            pool.dma_start(rows[:], row[0]).then_inc(ld_rows, 16)
            pool.wait_ge(mxl_done, KT)
            pool.wait_ge(x_done, KT)
            pool.dma_start(cT[:], cin).then_inc(ld_ctx, 16)
            for l in range(L2):
                if l:
                    pool.wait_ge(mv_used, N_MV)
                    pool.dma_start(rows[:], row[l]).then_inc(ld_rows, 16)
                pool.dma_start(wsT[:], sgw[l]).then_inc(ld_sg, 16)
                pool.dma_start(bsg[:], sgb[l]).then_inc(ld_sg, 16)

        @block.tensor
        def _(pe):
            def gemm(n, s, rhs, first=False):
                pe.wait_ge(w_hi, n + 1)
                pe.wait_ge(w_lo, n + 1)
                wh = whi[s][:].rearrange("p (k c f) -> p k c f", k=KT, f=P)
                wl = wlo[s][:].rearrange("p (k c f) -> p k c f", k=KT, f=P)
                for c in range(2):
                    if not first:
                        pe.wait_ge(acc_free[c], n)
                    for k in range(KT):
                        for w, part in ((wh, 0), (wh, 1), (wl, 0)):
                            for r in rhs:
                                last = pe.matmul(acc[:, c, r[2]:r[2] + r[3]], w[:, k, c, :], r[part][:, k, :],
                                                 start=(k == 0 and w is wh and part == 0),
                                                 stop=(k == KT - 1 and w is wl))
                    last.then_inc(acc_ready[c], 1)

            def matvec(s, landed, out_, rhs):
                pe.wait_ge(mv_loaded[s], landed)
                for k in range(KT):
                    last = pe.matmul(out_, mvr[:, s, k, :], rhs(k), start=(k == 0), stop=(k == KT - 1))
                last.then_inc(mv_used, 1)

            def norm_sums(q, segs, dg):
                pe.wait_ge(n_sq, q.sq + KT * len(segs))
                blocks = [(sq, o) for sq, w in segs for o in range(0, w, P)]
                for j, (sq, o) in enumerate(blocks):
                    for k in range(KT):
                        last = pe.matmul(ps_st[:, j:j + 1], sq[:, k, o:o + P], ones[:, 0:1],
                                         start=(k == 0), stop=(k == KT - 1))
                last.then_inc(n_st, 1)
                pe.wait_ge(n_dg, q.n + 1)
                for j in range(len(blocks)):
                    last = pe.matmul(bcast[:, j * P:(j + 1) * P], ones, dg[:, j, :], start=True, stop=True)
                last.then_inc(n_bc, 1)

            HX = [(hxh, hxl, 0, T)]
            pe.wait_ge(ld_small, N_SMALL)
            pe.wait_ge(silu_c, 1)
            for n in range(M1):
                matvec(n % MV_RING, 16 * (n // MV_RING + 1), ps_mv[:, n:n + 1], lambda k: sc1[:, k:k + 1])
            norm_sums(n_pre, [(nsq, T)], ndg)
            pe.wait_ge(n_out, n_pre.t + KT)
            gemm(0, 0, HX, first=True)
            gemm(1, 1, HX)
            with pe.Fori(1, (N_U + N_GL) // 2) as i:
                for s in range(2):
                    gemm(2 * i + s, s, HX)
            pe.wait_ge(silu_c, 2)

            def merge(i):
                for s in range(2):
                    gemm(C_MRG + 2 * i + s, s, HX)
                    pe.wait_ge(g_loaded[s], 16 * i + 16)
                    if not (isinstance(i, int) and i == 0 and s == 0):
                        pe.wait_ge(lru_ri, 4 * i + 2 * s)
                    for g in range(2):
                        last = pe.matmul(aux[:, 1 + g, :], wgate[:, s, g * P:(g + 1) * P], tile(uc, 2 * i + s),
                                         start=True, stop=True)
                    last.then_inc(lru_ps, 1)
                    for b in range(2 * MV_RING):
                        q = 2 * MV_RING * s + b
                        matvec(b % MV_RING, 16 * (4 * i + (M1 + q) // MV_RING + 1), tile(ps_mv.rearrange("p (a b) -> p a b", b=2), 12 * i + q),
                               lambda k: sc2[:, 2 * k:2 * k + 2])

            merge(0)
            with pe.Fori(1, N_MRG // 2) as i:
                merge(i)
            pe.wait_ge(lru_lo, KT)
            with pe.Fori(0, N_PB // 2) as i:
                for s in range(2):
                    gemm(C_PB + 2 * i + s, s, [(bh, bl, 0, T)])
            for hp in range(2):
                with pe.Fori(0, N_ATT // 2) as i:
                    for s in range(2):
                        gemm(C_ATT + hp * N_ATT + 2 * i + s, s, HX)
                attend(pe, hp)
            pe.wait_ge(atl_done, 4)
            for j in range(N_PA):
                n = C_PA + j
                pe.wait_ge(w_hi, n + 1)
                pe.wait_ge(w_lo, n + 1)
                wh = whi[j][:].rearrange("p (k c f) -> p k c f", k=4, f=P)
                wl = wlo[j][:].rearrange("p (k c f) -> p k c f", k=4, f=P)
                for c in range(4):
                    if c < 2:
                        pe.wait_ge(acc_free[c], n)
                    else:
                        pe.wait_ge(pa_free, 2 * j + c - 1)
                    for k in range(4):
                        pe.matmul(acc[:, c % 2, 0:T], wh[:, k, c, :], ath[:, k, :], start=(k == 0), stop=False)
                        pe.matmul(acc[:, c % 2, 0:T], wh[:, k, c, :], atl[:, k, :], start=False, stop=False)
                        last = pe.matmul(acc[:, c % 2, 0:T], wl[:, k, c, :], ath[:, k, :], start=False,
                                         stop=(k == 3))
                    last.then_inc(pa_ready if c < 2 else acc_ready[c % 2], 1)
            pe.wait_ge(mxl_done, KT)
            with pe.Fori(0, N_WO // 2) as i:
                for s in range(2):
                    gemm(C_WO + 2 * i + s, s, HX)
            norm_sums(n_post, [(nsq, T)], ndg)
            for l in range(L2):
                layer(pe, l, gemm, matvec, norm_sums)
            norm_sums(n_fin, [(nsq2, T)], ndg2)

        @block.scalar
        def _(act):
            act.dma_start(vecs[:], vec).then_inc(ld_small, 16)
            act.dma_start(xT[:], xin).then_inc(ld_small, 16)
            act.dma_start(consts[:], cst).then_inc(ld_small, 16)
            act.dma_start(mask[:], msk).then_inc(ld_small, 16)

            def split(n, s, half, first=False):
                act.wait_ge(w_loaded[s], 16 * half + 16)
                if not first:
                    act.wait_ge(acc_ready[1], n - 1)
                act.activation(whi[s][:], raw[s][:], ACT.Copy).then_inc(w_hi, 1)

            def norm_squares(src, sq):
                for k in range(KT):
                    act.activation(sq[:, k, :], src[:, k, :], ACT.Square).then_inc(n_sq, 1)

            def norm_modulate2(q, l, part, segs):
                shift = lambda k, z: mod2[:, 2 * (3 * KT * part + k) + z:2 * (3 * KT * part + k) + z + 1]
                scale = lambda k, z: coef[part][:, 2 * k + z:2 * k + z + 1]
                i = 0
                for k in range(KT):
                    for hi, o, w, z in segs:
                        act.wait_ge(n_t, q.t + i + 1)
                        if k >= 2:
                            act.wait_ge(n_out, q.t + i - 2 * len(segs) + 1)
                        for dst in (nh2[:, k % 2, o:o + w], hi[:, k, :]):
                            act.activation(dst, nt2[:, k % 2, o:o + w], ACT.Identity,
                                           bias=shift(k, z), scale=scale(k, z)).then_inc(n_h, 1)
                        i += 1

            def norm_root(q):
                act.wait_ge(n_var, q.n + 1)
                act.activation(sdc[:, 0:q.w // P], varc[:, 0:q.w // P], ACT.Sqrt).then_inc(n_sd, 1)

            def norm_modulate(q, scale, shift, hi):
                for k in range(KT):
                    act.wait_ge(n_t, q.t + k + 1)
                    if k >= 2:
                        act.wait_ge(n_out, q.t + k - 1)
                    act.activation(nh_[:, k % 2, 0:q.w], nt_[:, k % 2, 0:q.w], ACT.Identity,
                                   bias=shift(k), scale=scale(k)).then_inc(n_h, 1)
                    act.activation(hi[:, k, :], nt_[:, k % 2, 0:q.w], ACT.Identity,
                                   bias=shift(k), scale=scale(k)).then_inc(n_h, 1)

            act.wait_ge(ld_small, N_SMALL)
            act.activation(sc1, vcol("c"), ACT.Silu).then_inc(silu_c, 1)
            act.activation(sc2, vcol("cc"), ACT.Silu).then_inc(silu_c, 1)
            norm_squares(xT, nsq)
            for s in range(2):
                split(s, s, 0, first=True)
            act.activation(l_abs, vcol("lru"), ACT.Abs).then_inc(lru_e, 1)
            act.wait_ge(lru_e, 1)
            act.activation(l_e, l_abs, ACT.Exp, scale=-1.0).then_inc(lru_e, 1)
            norm_root(n_pre)
            act.wait_ge(mod_cols, 1)
            norm_modulate(n_pre, lambda k: a1[:, k:k + 1], lambda k: mod1[:, k:k + 1], hxh)
            with act.Fori(0, N_U // 2) as i:
                for s in range(2):
                    for c in range(2):
                        t = 2 * s + c
                        act.wait_ge(acc_ready[c], 2 * i + s + 1)
                        act.activation(tile(uc, 4 * i + t), acc[:, c, 0:T], ACT.Identity,
                                       bias=vecs[:, bass.ds(4 * i + (VOFF["conv_b"][0] + t), 1)],
                                       scale=vecs[:, bass.ds(16 * i + (VOFF["conv_w"][0] + 4 * t), 1)]
                                       ).then_inc(u_tap0, 1)
                    split(2 * i + s + 2, s, i + 1)
            act.preload_act_table(ACT.Silu)
            with act.Fori(0, N_GL // 2) as i:
                for s in range(2):
                    for c in range(2):
                        act.wait_ge(acc_ready[c], 2 * i + s + C_GL + 1)
                        act.activation(tile(sg, 4 * i + 2 * s + c), acc[:, c, 0:T], ACT.Silu
                                       ).then_inc(acc_free[c], 1)
                    split(2 * i + s + C_GL + 2, s, i + C_GL // 2 + 1)
            act.wait_ge(lru_sp, 1)
            with act.Fori(0, N_MRG // 2) as i:
                for s in range(2):
                    j = 2 * i + s
                    for c in range(2):
                        act.wait_ge(acc_ready[c], j + C_MRG + 1)
                        act.activation(tile(gates, 4 * i + 2 * s + c), acc[:, c, 0:T], ACT.Sigmoid
                                       ).then_inc(acc_free[c], 1)
                    split(j + C_MRG + 2, s, i + C_MRG // 2 + 1)
                    act.wait_ge(lru_ps, j + 1)
                    for g, (dst, b) in enumerate(((r_, "b_rg"), (i_, "b_ig"))):
                        act.activation(dst, aux[:, 1 + g, :], ACT.Sigmoid,
                                       bias=vecs[:, bass.ds(j + VOFF[b][0], 1)]).then_inc(lru_ri, 1)
                    act.wait_ge(lru_ri, 2 * j + 2)

                    act.activation(tau, r_, ACT.Tanh, scale=small[:, bass.ds(j + sp0, 1)]).then_inc(lru_ta, 1)
                    act.activation(a_, r_, ACT.Exp, scale=small[:, bass.ds(j + (sp0 + KT), 1)]).then_inc(lru_ta, 1)
                    act.wait_ge(lru_z, j + 1)
                    act.activation(z_, z_, ACT.Sqrt).then_inc(lru_sq, 1)
                    act.wait_ge(lru_out, j + 1)
                    act.activation(tile(bh, j), x_, ACT.Copy).then_inc(lru_hi, 1)
            with act.Fori(0, N_PB // 2) as i:
                for s in range(2):
                    split(2 * i + s + C_PB + 2, s, i + C_PB // 2 + 1)
            for hp in range(2):
                n0 = C_ATT + hp * N_ATT
                act.wait_ge(acc_ready[0], n0 + 1)
                with act.Fori(0, N_ATT // 2 - 1) as i:
                    for s in range(2):
                        n = 2 * i + s + n0
                        act.wait_ge(acc_ready[0], n + 1)
                        act.activation(tile(qkvg, 4 * i + 2 * s), acc[:, 0, 0:T], ACT.Copy).then_inc(acc_free[0], 1)
                        split(n + 2, s, i + n0 // 2 + 1)
                for s in range(2):
                    n = n0 + N_ATT - 2 + s
                    for c in range(2):
                        if s == 0 and c == 1:
                            continue
                        act.wait_ge(acc_ready[c], n + 1)
                        act.activation(qkvg[:, 2 * (N_ATT - 2 + s) + c, :], acc[:, c, 0:T],
                                       ACT.Silu if s else ACT.Copy).then_inc(acc_free[c], 1)
                    split(n + 2, s, n // 2 + 1)
                attend_act(act, hp)
            act.wait_ge(at_out, 16)
            for k in range(4):
                act.activation(ath[:, k, :], att[:, k, :], ACT.Copy).then_inc(ath_done, 1)
            for j in range(N_PA):
                for c in range(4):
                    t = 4 * j + c
                    act.wait_ge(mix_done, t + 1)
                    act.activation(hxh[:, t, :], mix[:, t, :], ACT.Copy).then_inc(mxh_done, 1)
                split(C_PA + j + 2, j, C_PA // 2 + 1)
            for j in range(N_WO):
                n = C_WO + j
                for c in range(2):
                    act.wait_ge(acc_ready[c], n + 1)
                    act.activation(nsq[:, 2 * j + c, :], acc[:, c, 0:T], ACT.Square).then_inc(n_sq, 1)
                split(n + 2, n % 2, n // 2 + 1)
            norm_root(n_post)
            for l in range(L2):
                layer_act(act, l, split, norm_squares, norm_root, norm_modulate2)
            act.wait_ge(acc_ready[1], N_CHUNKS)
            for k in range(KT):
                act.wait_ge(acc_free[k % 2], N_CHUNKS - 4 + k // 2 + 1)
                act.activation(nsq2[:, k, :], xT[:, k, :], ACT.Square).then_inc(n_sq, 1)
            norm_root(n_fin)

        @block.vector
        def _(dve):
            chain = Chain(dve, dve_step)
            link = chain.link

            def split(n, s):
                dve.wait_ge(w_hi, n + 1)
                dve.tensor_tensor(wlo[s][:], raw[s][:], whi[s][:].bitcast(F32), ALU.subtract).then_inc(w_lo, 1)

            def norm_scale(q, dg):
                nj = q.w // P
                dve.wait_ge(n_st, q.n + 1)
                dve.tensor_scalar(varc[:, 0:nj], ps_st[:, 0:nj], 1.0 / D, EPS, ALU.mult, ALU.add).then_inc(n_var, 1)
                dve.wait_ge(n_sd, q.n + 1)
                link(dve.reciprocal(rsc[:, 0:nj], sdc[:, 0:nj]))
                for j in range(nj):
                    last = dve.tensor_scalar(dg[:, j, :], ident, rsc[:, j:j + 1], None, ALU.mult)
                last.then_inc(n_dg, 1)
                dve.wait_ge(n_bc, q.n + 1)

            def norm_modulate2(q, segs):
                i = 0
                for k in range(KT + 1):
                    for j, (src, hi, lo, o, w) in enumerate(segs):
                        if k < KT:
                            if k >= 2:
                                dve.wait_ge(n_h, 2 * (q.t + (k - 2) * len(segs) + j + 1))
                            dve.tensor_tensor(nt2[:, k % 2, o:o + w], src[:, k, :], bcast[:, o:o + w], ALU.mult
                                              ).then_inc(n_t, 1)
                    for j, (src, hi, lo, o, w) in enumerate(segs):
                        if k > 0:
                            dve.wait_ge(n_h, 2 * (q.t + (k - 1) * len(segs) + j + 1))
                            dve.tensor_tensor(lo[:, k - 1, :], nh2[:, (k - 1) % 2, o:o + w],
                                              hi[:, k - 1, :].bitcast(F32), ALU.subtract).then_inc(n_out, 1)

            def norm_modulate(q, src, hi, lo):
                for k in range(KT + 1):
                    if k < KT:
                        if k >= 2:
                            dve.wait_ge(n_h, 2 * (q.t + k - 1))
                        dve.tensor_tensor(nt_[:, k % 2, 0:q.w], src[:, k, :], aux[:, 1, 0:q.w], ALU.mult
                                          ).then_inc(n_t, 1)
                    if k > 0:
                        dve.wait_ge(n_h, 2 * (q.t + k))
                        dve.tensor_tensor(lo[:, k - 1, :], nh_[:, (k - 1) % 2, 0:q.w],
                                          hi[:, k - 1, :].bitcast(F32), ALU.subtract).then_inc(n_out, 1)

            for c in range(2):
                dve.memset(lam_p[:, c:c + 1], 0.0).then_inc(f_sq, 1)
            dve.wait_ge(ld_small, N_SMALL)
            for s in range(2):
                split(s, s)
            dve.wait_ge(lru_e, 2)
            link(dve.tensor_scalar(l_z2, l_e, 2.0, None, ALU.add))
            link(dve.reciprocal(l_z, l_z2))
            link(dve.tensor_tensor(l_z, l_z, l_e, ALU.mult))
            link(dve.tensor_tensor(l_z2, l_z, l_z, ALU.mult))
            link(dve.tensor_scalar(l_q, l_z2, 1.0 / 19, None, ALU.mult))
            for d in range(17, 1, -2):
                link(dve.scalar_tensor_tensor(l_q, l_q, 1.0 / d, l_z2, ALU.add, ALU.mult))
            link(dve.scalar_tensor_tensor(l_q, l_q, 1.0, l_z, ALU.add, ALU.mult))
            link(dve.tensor_scalar(l_m, vcol("lru"), -8.0, 0.0, ALU.mult, ALU.max))
            link(dve.scalar_tensor_tensor(sp, l_q, 16.0, l_m, ALU.mult, ALU.add))
            dve.tensor_scalar(nsp, sp, -1.0, None, ALU.mult).then_inc(lru_sp, 1)

            dve.wait_ge(mv_used, M1)
            link(dve.tensor_tensor(mod1, ps_mv[:, 0:M1], vcol("b_mod"), ALU.add))
            link(dve.tensor_tensor(r1, mod1[:, 2 * KT:3 * KT], vcol("g_post"), ALU.mult))
            dve.scalar_tensor_tensor(a1, mod1[:, KT:2 * KT], 1.0, vcol("g_pre"), ALU.add, ALU.mult
                                     ).then_inc(mod_cols, 1)
            norm_scale(n_pre, ndg)
            norm_modulate(n_pre, xT, hxh, hxl)
            with chain.loop(N_U // 2, 8) as i:
                for s in range(2):
                    for c in range(2):
                        t = 2 * s + c
                        dve.wait_ge(u_tap0, 4 * i + t + 1)
                        for tap in range(1, 4):
                            o = tile(uc, 4 * i + t)[:, tap:T]
                            ins = dve.scalar_tensor_tensor(
                                o, acc[:, c, 0:T - tap], vecs[:, bass.ds(16 * i + (VOFF["conv_w"][0] + 4 * t + tap), 1)],
                                o, ALU.mult, ALU.add)
                            if tap < 3:
                                link(ins)
                            else:
                                ins.then_inc(acc_free[c], 1)
                    split(2 * i + s + 2, s)
            with dve.Fori(0, N_GL // 2) as i:
                for s in range(2):
                    split(2 * i + s + C_GL + 2, s)
            with chain.loop(N_MRG // 2, 8) as i:
                for s in range(2):
                    j = 2 * i + s
                    split(j + C_MRG + 2, s)
                    dve.wait_ge(lru_ta, 2 * j + 2)
                    link(dve.tensor_tensor(z_, a_, a_, ALU.mult))
                    dve.scalar_tensor_tensor(z_, z_, 1.0, tau, ALU.add, ALU.mult).then_inc(lru_z, 1)
                    link(dve.tensor_tensor(x_, i_, tile(uc, j), ALU.mult))
                    dve.wait_ge(lru_sq, j + 1)
                    link(dve.tensor_tensor(x_, x_, z_, ALU.mult))
                    link(dve.tensor_tensor_scan(h_, a_, x_, 0.0, ALU.mult, ALU.add))
                    dve.tensor_tensor(x_, h_, tile(sg, j), ALU.mult).then_inc(lru_out, 1)
                    dve.wait_ge(lru_hi, j + 1)
                    dve.tensor_tensor(tile(bl, j), x_, tile(bh, j).bitcast(F32), ALU.subtract).then_inc(lru_lo, 1)
            dve.wait_ge(mv_used, M1 + M2)
            dve.tensor_tensor(mod2, ps_mv, vcol("ada_b0"), ALU.add).then_inc(mod_cols, 1)
            with dve.Fori(0, N_PB // 2) as i:
                for s in range(2):
                    for c in range(2):
                        dve.wait_ge(acc_ready[c], 2 * i + s + C_PB + 1)
                        g = tile(gates, 4 * i + (KT + 2 * s + c))
                        dve.tensor_tensor(g, acc[:, c, 0:T], g, ALU.mult).then_inc(acc_free[c], 1)
                    split(2 * i + s + C_PB + 2, s)
            for hp in range(2):
                n0 = C_ATT + hp * N_ATT
                with dve.Fori(0, N_ATT // 2 - 1) as i:
                    for s in range(2):
                        n = 2 * i + s + n0
                        dve.wait_ge(acc_ready[1], n + 1)
                        dve.tensor_copy(tile(qkvg, 4 * i + 2 * s + 1), acc[:, 1, 0:T]).then_inc(acc_free[1], 1)
                        split(n + 2, s)
                n = n0 + N_ATT - 2
                dve.wait_ge(acc_ready[1], n + 1)
                dve.tensor_copy(qkvg[:, 2 * (N_ATT - 2) + 1, :], acc[:, 1, 0:T]).then_inc(acc_free[1], 1)
                split(n + 2, 0)
                split(n + 3, 1)
                attend_dve(dve, link, hp)
            for k in range(4):
                dve.wait_ge(ath_done, k + 1)
                dve.tensor_tensor(atl[:, k, :], att[:, k, :], ath[:, k, :].bitcast(F32), ALU.subtract
                                  ).then_inc(atl_done, 1)
            for j in range(N_PA):
                for c in range(4):
                    t = 4 * j + c
                    dve.wait_ge(pa_ready if c < 2 else acc_ready[c % 2], 2 * j + c + 1 if c < 2 else C_PA + j + 1)
                    ins = dve.tensor_tensor(nt_[:, t % 2, :], acc[:, c % 2, 0:T], gate_a[:, t, :], ALU.mult)
                    ins.then_inc(pa_free if c < 2 else acc_free[c % 2], 1)
                    dve.wait_ge(pa_free if c < 2 else acc_free[c % 2], 2 * j + c + 1 if c < 2 else C_PA + j + 1)
                    dve.tensor_tensor(mix[:, t, :], mix[:, t, :], nt_[:, t % 2, :], ALU.add).then_inc(mix_done, 1)
                    dve.wait_ge(mxh_done, t + 1)
                    dve.tensor_tensor(hxl[:, t, :], mix[:, t, :], hxh[:, t, :].bitcast(F32), ALU.subtract
                                      ).then_inc(mxl_done, 1)
                split(C_PA + j + 2, j)
            for j in range(N_WO):
                n = C_WO + j
                for c in range(2):
                    dve.wait_ge(n_sq, n_post.sq + 2 * j + c + 1)
                    dve.tensor_copy(o32[:, 2 * j + c, :], acc[:, c, 0:T]).then_inc(acc_free[c], 1)
                split(n + 2, n % 2)
            norm_scale(n_post, ndg)
            for k in range(KT):
                link(dve.tensor_tensor(nt_[:, k % 2, :], o32[:, k, :], aux[:, 1, :], ALU.mult))
                dve.scalar_tensor_tensor(xT[:, k, :], nt_[:, k % 2, :], r1[:, k:k + 1], xT[:, k, :],
                                         ALU.mult, ALU.add).then_inc(x_done, 1)
            for l in range(L2):
                layer_dve(dve, link, l, split, norm_scale, norm_modulate2, chain)
            norm_scale(n_fin, ndg2)
            for k in range(KT):
                dve.scalar_tensor_tensor(xT[:, k, :], xT[:, k, :], vcol("final_g", k, 1), bcast[:, 0:T],
                                         ALU.mult, ALU.mult).then_inc(x_done, 1)


def _cols(a):
    return np.reshape(a, (-1, P)).T


def _chunk(w, kt):
    return np.reshape(w, (kt, P, -1)).transpose(1, 0, 2).reshape(P, -1)


def _columns(w, width):
    return [_chunk(w[:, c:c + width], w.shape[0] // P) for c in range(0, w.shape[1], width)]


def layout(inp):
    w_in = inp["w_in"][0]
    att, u0 = 9 * 512 + 512, 9 * 512 + 512
    chunks = _columns(w_in[:, u0:], CW)
    chunks += _columns(inp["w_pb"][0], CW)
    for hp in range(2):
        for j in range(N_ATT):
            c = 512 * j + CW * hp
            chunks.append(_chunk(w_in[:, c:c + CW], KT))
    chunks += _columns(inp["w_pa"][0], 2 * CW)
    chunks += _columns(inp["w_o"][0], CW)
    mv = _columns(inp["w_mod"][0], P)
    for l in range(L2):
        chunks += _columns(inp["w_in_2"][l], CW)
        chunks += _columns(inp["w_out_2"][l], CW)
        for b in range(NFB):
            chunks += _columns(inp["mlp_w1_2"][l][:, b * D:(b + 1) * D], CW)
            chunks += _columns(inp["mlp_w2_2"][l][b * D:(b + 1) * D], CW)
        mv += _columns(inp["ada_w_2"][l], P)
    assert len(chunks) == N_CHUNKS and len(mv) == N_MV

    def pair(a, b):
        return np.stack([_cols(a), _cols(b)], 2).reshape(P, -1)

    v = {"c": _cols(inp["c"][0]), "cc": pair(inp["c_2"][0], inp["c_ctx_2"]), "b_mod": _cols(inp["b_mod"][0]),
         "g_pre": _cols(inp["g_pre"][0]),
         "conv_w": np.reshape(inp["conv_w"][0], (4, KT, P)).transpose(2, 1, 0).reshape(P, -1),
         "conv_b": _cols(inp["conv_b"][0]), "b_rg": _cols(inp["b_rg"][0]), "b_ig": _cols(inp["b_ig"][0]),
         "lru": _cols(inp["lru_lambda"][0]), "g_post": _cols(inp["g_post"][0]), "final_g": _cols(inp["final_g_2"])}
    for l in range(L2):
        g = {"ada_b": "ada_b_2", "n1g": "norm1_g_2", "n2g": "norm2_g_2"}
        for k, name in g.items():
            v[f"{k}{l}"] = pair(inp[name][l], inp[name][l])
        v[f"caw{l}"] = np.reshape(inp["conv_a_w_2"][l], (TAPS_A, 2, P)).transpose(2, 1, 0).reshape(P, -1)
        v[f"cdw{l}"] = np.reshape(inp["conv_d_w_2"][l], (3, 2, P)).transpose(2, 1, 0).reshape(P, -1)
        for k, name in {"cab": "conv_a_b_2", "lag": "ln_a_g_2", "lab": "ln_a_b_2", "sgg": "sg_ln_g_2",
                        "sgb": "sg_ln_b_2"}.items():
            v[f"{k}{l}"] = _cols(inp[name][l])
    vec = np.concatenate([v[n] for n, _ in VECS], 1)
    assert vec.shape == (P, NV)

    gst = np.zeros((KT, P, 2, P), np.float32)
    for j in range(KT):
        for b in range(2):
            s = slice(64 * b, 64 * b + 64)
            gst[j, s, 0, s] = inp["w_rg"][0, 2 * j + b]
            gst[j, s, 1, s] = inp["w_ig"][0, 2 * j + b]
    x = np.reshape(inp["x"][0].T, (KT, P, T)).transpose(1, 0, 2)
    c = np.reshape(inp["ctx_2"][0].T, (KT, P, TC)).transpose(1, 0, 2)
    return {"wst": np.stack(chunks), "mst": np.stack(mv), "vec": vec, "xin": x, "cin": c,
            "gst": gst.reshape(KT, P, 2 * P), **layer_inputs(inp), **tables()}


def layer_inputs(inp):
    rows, sgw, sgb = [], [], []
    for l in range(L2):
        r = np.concatenate([inp["subln_g_2"][l]] + [inp[f"lam_{n}_2"][l] for n in ("q1", "k1", "q2", "k2")])
        rows.append(np.broadcast_to(r, (P, 192)))
        sgw.append(inp["sg_w_2"][l].transpose(2, 0, 1))
        sgb.append(np.repeat(np.reshape(inp["sg_b_2"][l], (2, 2, P)), 64, axis=1).transpose(1, 0, 2))
    return {"row": np.stack(rows), "sgw": np.stack(sgw), "sgb": np.stack(sgb)}


def tables():
    ident = np.eye(P, dtype=np.float32)
    ones = np.ones((P, P), np.float32)
    f = np.arange(P)
    partner = np.where(f % 16 < 8, f + 8, f - 8)
    perm = np.zeros((P, P), np.float32)
    perm[partner, f] = np.where(f % 16 < 8, -1.0, 1.0)
    cst = np.concatenate([ident, ones, perm, np.full((P, P), 1.0 / GW, np.float32)], 1)
    i = np.arange(P)[:, None]
    dist = 4 * i - (np.arange(T + 3)[None, :] - 3)
    band = np.where((dist >= 0) & (dist <= 128), 0.0, NEG)
    j = np.arange(P)[None, :]
    g1 = np.where(j <= i, 0.0, NEG)
    g2 = np.where((j <= i) & ((i - j) % 4 == 0), 0.0, NEG)
    msk = np.concatenate([band, np.zeros((P, 1)), g1, g2], 1).astype(np.float32)
    tok = np.arange(T)
    inv = np.float32(10000.0) ** (-np.arange(0, 16, 2, dtype=np.float32) / np.float32(16))
    pos = np.where(f[:, None] % 32 < 16, tok[None, :] // 64, tok[None, :] % 64).astype(np.float32)
    angle = pos * inv[f % 8][:, None]
    return {"cst": cst, "msk": msk, "rop": np.stack([np.cos(angle), np.sin(angle)], 1).astype(np.float32)}


_INS = ["wst", "mst", "vec", "xin", "cin", "gst", "cst", "msk", "rop", "row", "sgw", "sgb"]


def kernel(**inputs):
    import concourse.bacc as bacc
    from concourse.bass_utils import run_bass_kernel_spmd

    nc = bacc.Bacc("TRN2", target_bir_lowering=False, num_devices=1)
    data = layout(inputs)
    arrays, args = {}, []
    for name in _INS:
        a = np.ascontiguousarray(data[name])
        arrays[f"in_{name}"] = a
        args.append(nc.dram_tensor(f"in_{name}", a.shape, mybir.dt.from_np(a.dtype), kind="ExternalInput").ap())
    out = nc.dram_tensor("out_x", (P, KT, T), F32, kind="ExternalOutput").ap()
    build(nc, *args, out)
    r = run_bass_kernel_spmd(nc, [arrays], core_ids=[0])
    got = r.results[0]["out_x"]
    return np.ascontiguousarray(got.transpose(1, 0, 2).reshape(D, T).T)[None]
```

```python
import math
from contextlib import ExitStack

import numpy as np

import concourse.bass as bass
from concourse import mybir

F32 = mybir.dt.float32
F32R = mybir.dt.float32r
ACT = mybir.ActivationFunctionType
ALU = mybir.AluOpType
AX_X = mybir.AxisListType.X

P = 128
D = 1024
KT = D // P
T = 512
TC = 256
DH = 128
EPS = 1e-6
TX = T + TC
NEG = -1e30
CW = 256
WF = KT * CW
L2 = 2
GW = 256
TAPS_A = 31
FF = 4096
NFB = FF // D
XPA = TX + 60
XPD = TX + 4
CONV_STEPS = 2 * TAPS_A
QSCALE = 32 ** -0.5
W_IN_ORDER = (0, 1, 2, 3, 4, 8, 9, 7, 5, 6)
SEL = 9 * 32
N_SMALL = 3 * 16

N_U, N_GL, N_MRG, N_PB, N_ATT, N_PA, N_WO = 4, 4, 8, 4, 10, 2, 4
C_U = 0
C_GL = C_U + N_U
C_MRG = C_GL + N_GL
C_PB = C_MRG + N_MRG
C_ATT = C_PB + N_PB
C_PA = C_ATT + 2 * N_ATT
C_WO = C_PA + N_PA
C_L = C_WO + N_WO
N_WIN, N_WOUT, N_FF = 10, 4, 8 * NFB
N_L = N_WIN + N_WOUT + N_FF
N_CHUNKS = C_L + L2 * N_L
MW = 512
G1, G2 = 3 * D // MW, 6 * D // MW
N_G = G1 + L2 * G2
M1, M2 = 3 * KT, 6 * KT
MV_RING = 4
KX = 2
KC = KT - KX
FF_MV = (0, 1, None, 2, 3, 4, 5, None)
FF_SUMS = (2, 5, 7)

VECS = [("c", 8), ("cc", 16), ("b_mod", 24), ("g_pre", 8), ("conv_w", 32), ("conv_b", 8),
        ("b_rg", 8), ("b_ig", 8), ("lru", 8), ("g_post", 8), ("final_g", 8)]
for _l in range(L2):
    VECS += [(f"ada_b{_l}", 96), (f"n1g{_l}", 16), (f"n2g{_l}", 16), (f"caw{_l}", 2 * TAPS_A),
             (f"cab{_l}", 2), (f"lag{_l}", 2), (f"lab{_l}", 2), (f"sgg{_l}", 2), (f"sgb{_l}", 2),
             (f"cdw{_l}", 6)]
VOFF, NV = {}, 0
for _n, _k in VECS:
    VOFF[_n] = (NV, _k)
    NV += _k


def ceil32(n):
    return (n + 31) // 32 * 32


class Map:

    def __init__(self, nc, base):
        self.nc, self.base = nc, ceil32(base)

    def at(self, name, shape, kb, dt=F32):
        n = 4
        for s in shape[1:]:
            n *= s
        assert self.base + int(kb * 1024) + n <= self.nc.sbuf_usable_end, name
        return self.nc.alloc_sbuf_tensor_at(name, list(shape), dt, offset=self.base + int(kb * 1024))



class Chain:

    def __init__(self, eng, sem):
        self.eng, self.sem, self.n, self.regs = eng, sem, 0, []

    def link(self, ins):
        ins.then_inc(self.sem, 1)
        self.n += 1
        value = self.n
        for reg, per in self.regs:
            value = reg * per + value
        self.eng.wait_ge(self.sem, value)

    def loop(self, count, per):
        return _ChainLoop(self, count, per)


class _ChainLoop:
    def __init__(self, chain, count, per):
        self.chain, self.count, self.per = chain, count, per

    def __enter__(self):
        self.start = self.chain.n
        self.fori = self.chain.eng.Fori(0, self.count)
        reg = self.fori.__enter__()
        self.chain.regs.append((reg, self.per))
        return reg

    def __exit__(self, *e):
        self.chain.regs.pop()
        self.fori.__exit__(*e)
        assert e[0] or self.chain.n - self.start == self.per, self.chain.n - self.start
        self.chain.n = self.start + self.per * self.count


class Norm:

    def __init__(self, all_, modulates, w=T):
        self.n, self.w = len(all_), w
        self.segs = 2 if w > T else 1
        self.sq = sum(KT * q.segs for q in all_)
        self.t = sum(KT * q.segs for q in all_ if q.mod)
        self.mod = modulates
        all_.append(self)


def tile(ap, i):
    return ap[:, bass.ds(i, 1), :].rearrange("p o t -> p (o t)")


def build(nc, wst, mst, vec, xin, cin, gst, cst, msk, rop, seli, row, sgw, sgb, out):
    with ExitStack() as ctx:
        m = Map(nc, nc.sbuf_base)

        def sem(name):
            return ctx.enter_context(nc.semaphore(name))

        raw = [m.at(f"raw{s}", [P, WF], 8 * s) for s in range(2)]
        whi = [m.at(f"whi{s}", [P, WF], 16 + 8 * s, F32R) for s in range(2)]
        wlo = [m.at(f"wlo{s}", [P, WF], 32 + 8 * s, F32R) for s in range(2)]
        mvr = m.at("mvr", [P, MV_RING, MW], 48)
        macc = m.at("macc", [P, 2, MW], 56)
        xT = m.at("xT", [P, KT, T], 60)
        cT = m.at("cT", [P, KT, TC], 76)
        vecs = m.at("vecs", [P, NV], 84)
        consts = m.at("consts", [P, 4 * P], 86.5)
        ident, ones, perm = consts[:, 0:P], consts[:, P:2 * P], consts[:, 2 * P:3 * P]
        avg = consts[:, 3 * P:4 * P]
        small = m.at("small", [P, 512], 88.5)
        mask = m.at("mask", [P, 772], 90.5)
        hxh = m.at("hxh", [P, KT, T], 96, F32R)
        hxl = m.at("hxl", [P, KT, T], 112, F32R)

        def vcol(name, j=0, n=None):
            o, k = VOFF[name]
            return vecs[:, o + j:o + (k if n is None else j + n)]

        cols = [0]

        def scol(n):
            cols[0] += n
            return small[:, cols[0] - n:cols[0]]

        sc1, sc2 = scol(8), scol(16)
        mod1 = scol(24)
        a1, r1 = scol(8), scol(8)
        sp0 = cols[0]
        sp, nsp = scol(8), scol(8)
        l_abs, l_e, l_z, l_z2, l_q, l_m = (scol(8) for _ in range(6))
        varc, sdc, rsc = scol(8), scol(8), scol(8)
        nmx, lsum, rsum = scol(2), scol(2), scol(2)
        mod2_0 = cols[0]
        mod2 = scol(2 * M2)
        coef = [scol(16), scol(16)]
        scr = scol(64)
        lam_p, lam_x, lamc = scol(2), scol(2), scol(1)
        dnm, dls, drs = scol(4), scol(4), scol(8)
        oss, osd, ors = scol(24), scol(24), scol(24)

        acc = ctx.enter_context(nc.psum_tensor("acc", [P, 2, 1024], F32))
        aux = ctx.enter_context(nc.psum_tensor("aux", [P, 4, 512], F32))
        ps_mv = aux[:, 0, 0:96]
        ps_st = aux[:, 3, 0:8]
        auxf = aux[:].rearrange("p a b -> p (a b)")
        bcast = aux[:, 1:3, :].rearrange("p a b -> p (a b)")

        gates = m.at("gates", [P, 2 * KT, T], 128)
        gate_a = gates[:, 0:KT, :]
        mix = gates[:, KT:2 * KT, :]
        uc = m.at("uc", [P, KT, T], 160)
        sg = m.at("sg", [P, KT, T], 176)
        bh = m.at("bh", [P, KT, T], 160, F32R)
        bl = m.at("bl", [P, KT, T], 176, F32R)
        lr = m.at("lr", [P, 6, T], 192)
        mprod = [m.at("mprod0", [P, MW], 204), m.at("mprod1", [P, MW], 204.5)]
        r_, i_, tau, a_, z_, x_ = (lr[:, k, :] for k in range(6))
        wgate = m.at("wgate", [P, 2, 2 * P], 76)
        qkvg = m.at("qkvg", [P, 2 * N_ATT, T], 160)
        att = m.at("att", [P, 4, T], 76)
        vn = m.at("vn", [P, 12, P], 200)
        s_sb = m.at("s_sb", [P, 2, 768], 48)
        pt = m.at("pt", [P, 2, 768], 54)
        ath = m.at("ath", [P, 4, T], 160, F32R)
        atl = m.at("atl", [P, 4, T], 168, F32R)
        o32 = m.at("o32", [P, KT, T], 176)
        nsq = m.at("nsq", [P, KT, T], 160)
        nt_ = m.at("nt_", [P, 2, T], 192)
        nh_ = m.at("nh_", [P, 2, T], 196)
        ndg = m.at("ndg", [P, 4, P], 200)

        hch = m.at("hch", [P, KT, TC], 128, F32R)
        hcl = m.at("hcl", [P, KT, TC], 136, F32R)
        rope = m.at("rope", [P, 2, T], 90.5)
        rows = m.at("rows", [P, 192], 95.25)
        nsq2 = m.at("nsq2", [P, KT, T], 144)
        nsqc = m.at("nsqc", [P, KT, TC], 160)
        nt2 = m.at("nt2", [P, 2, TX], 168)
        nh2 = m.at("nh2", [P, 2, TX], 180)
        ndg2 = m.at("ndg2", [P, 6, P], 186)
        gpad = m.at("gpad", [P, 2, XPA], 144)
        aconv = m.at("aconv", [P, 2, XPA - 30], 150.5)
        qT = m.at("qT", [P, 2, TX], 156.75)
        kT = m.at("kT", [P, 2, TX], 162.75)
        vT = m.at("vT", [P, 2, TX], 168.75)
        vnat = m.at("vnat", [P, 6, GW], 174.75)
        av = m.at("av", [P, 2, TX], 174.75)
        ug = m.at("ug", [P, 2, TX], 180.75)
        svg = m.at("svg", [P, 2, TX], 186.75)
        bgt = m.at("bgt", [P, 2, TX], 192.75)
        cx = m.at("cx", [P, 2, XPD], 198.75)
        sigt = m.at("sigt", [P, 2, TX], 198.75)
        tmp = m.at("tmp", [P, TX], 204.8125)
        yca = m.at("yca", [P, 2, TX], 144)
        sqm = m.at("sqm", [P, 2, TX], 168.75)
        snat = m.at("snat", [P, 6, GW], 168.75)
        dconv = m.at("dconv", [P, XPD - 2], 54.5)
        wsT = m.at("wsT", [P, 4, P], 48)
        bsg = m.at("bsg", [P, 2, P], 50)
        ndm = m.at("ndm", [P, 6, P], 51)
        sel = m.at("sel", [P, 4 * SEL], 90.5)
        selr = m.at("selr", [P, 4 * SEL], 90.5, F32R)
        qlo = m.at("qlo", [P, 2, TX], 156.75, F32R)
        klo = m.at("klo", [P, 2, TX], 162.75, F32R)
        stack = [m.at(f"stack{b}", [P, 4, TX], 180.75 + 12 * b, F32R) for b in range(2)]
        prob = m.at("prob", [P, 2, 2, TX], 48)
        ptd = m.at("ptd", [P, 2, TX], 168.75)
        onat = m.at("onat", [P, 6, GW], 144)
        osq = m.at("osq", [P, 6, GW], 150.5)
        fxh = m.at("fxh", [P, KT, T], 144, F32R)
        fxl = m.at("fxl", [P, KT, T], 160, F32R)
        fch = m.at("fch", [P, KT, TC], 176, F32R)
        fcl = m.at("fcl", [P, KT, TC], 184, F32R)
        relu = m.at("relu", [P, 2, TX], 192)
        fsq = m.at("fsq", [P, 2, TX], 198)

        ld_small = sem("ld_small")
        w_loaded = [sem(f"w_loaded{s}") for s in range(2)]
        w_hi = sem("w_hi")
        w_lo = sem("w_lo")
        mv_loaded = [sem(f"mv_loaded{s}") for s in range(MV_RING)]
        mv_x, mv_c = sem("mv_x"), sem("mv_c")
        mv_p = sem("mv_p")
        mv_sum = sem("mv_sum")
        acc_ready = [sem(f"acc_ready{c}") for c in range(2)]
        acc_free = [sem(f"acc_free{c}") for c in range(2)]
        silu_c = sem("silu_c")
        mod_cols = sem("mod_cols")
        dve_step = sem("dve_step")
        n_ad = sem("norm_ad")
        n_sq, n_st, n_var, n_sd, n_dg, n_bc, n_t, n_h, n_out = (
            sem(f"norm_{x}") for x in ("sq", "st", "var", "sd", "dg", "bc", "t", "h", "out"))
        u_tap0 = sem("u_tap0")
        g_loaded = [sem(f"g_loaded{s}") for s in range(2)]
        lru_ps, lru_ri, lru_ta, lru_z, lru_sq, lru_out, lru_hi, lru_lo = (
            sem(f"lru_{x}") for x in ("ps", "ri", "ta", "z", "sq", "out", "hi", "lo"))
        lru_e, lru_sp = sem("lru_e"), sem("lru_sp")
        at_vt, at_vn, at_s, at_m, at_nm, at_e, at_p, at_t, at_pt, at_o, at_out = (
            sem(f"at_{x}") for x in ("vt", "vn", "s", "m", "nm", "e", "p", "t", "pt", "o", "out"))
        ath_done, atl_done = sem("ath_done"), sem("atl_done")
        pa_ready, pa_free = sem("pa_ready"), sem("pa_free")
        mix_done, mxh_done, mxl_done = sem("mix_done"), sem("mxh_done"), sem("mxl_done")
        x_done = sem("x_done")
        ld_ctx, ld_vec = sem("ld_ctx"), sem("ld_vec")
        ld_rope, ld_rows, ld_sg = sem("ld_rope"), sem("ld_rows"), sem("ld_sg")
        lam_s, lam_e, lam_ok = sem("lam_s"), sem("lam_e"), sem("lam_ok")
        glu, cx_zero, conv_step = sem("glu"), sem("cx_zero"), sem("conv_step")
        rot, roped = sem("rot"), sem("roped")
        v_t, v_nat = sem("v_t"), sem("v_nat")
        m_mean, m_cen, m_sq, m_st, m_var, m_sd, m_dg, m_bc, m_t, m_fin = (
            sem(f"ln_{x}") for x in ("mean", "cen", "sq", "st", "var", "sd", "dg", "bc", "t", "fin"))
        s_t, s_nat, s_mix, s_out, d_out = (sem(x) for x in ("sg_t", "sg_nat", "sg_mix", "sg_out", "d_out"))
        y_hi, y_lo = sem("y_hi"), sem("y_lo")
        q_s, q_m, q_e, q_w, q_t, q_pt, q_o, q_on = (
            sem(f"diff_{x}") for x in ("s", "m", "e", "w", "t", "pt", "o", "on"))
        o_sq, o_var, o_sd, o_n, o_t = (sem(f"sub_{x}") for x in ("sq", "var", "sd", "n", "t"))
        f_relu, f_hi, f_sq, f_lo = (sem(f"ff_{x}") for x in ("relu", "hi", "sq", "lo"))
        ld_sel, sel_ok = sem("ld_sel"), sem("sel_ok")
        qk_hi, qk_lo = sem("qk_hi"), sem("qk_lo")
        st_ps, st_act, st_dve = sem("stack_ps"), sem("stack_act"), sem("stack_dve")
        stored = sem("stored")

        norms = []
        n_pre = Norm(norms, True)
        n_post = Norm(norms, False)
        n_mix, n_ff = [], []
        for l in range(L2):
            n_mix.append(Norm(norms, True, TX))
            n_ff.append(Norm(norms, True, TX if l == 0 else T))
        n_fin = Norm(norms, False)
        assert [q.n for q in norms] == list(range(len(norms)))

        block = ctx.enter_context(nc.Block())

        def attend(pe, hp):
            base = 8 * hp
            for c in range(2):
                pe.wait_ge(acc_free[c], C_ATT + (hp + 1) * N_ATT)

            def scores(u):
                hh, r = (u // 4) % 2, u % 4
                if u >= base + 2:
                    pe.wait_ge(at_m, u - 1)
                for g in range(3):
                    q, k = qkvg[:, 2 * g + hh, r::4], qkvg[:, 6 + 2 * g + hh, :]
                    if g == 0:
                        pe.matmul(acc[:, u % 2, 0:T], q, k, start=True, stop=True)
                    else:
                        o = T + (g - 1) * P
                        last = pe.matmul(acc[:, u % 2, o:o + P], q, k[:, r::4], start=True, stop=True)
                last.then_inc(at_s, 1)

            def values(hh):
                head = 2 * hp + hh
                if head > 0:
                    pe.wait_ge(at_pt, 4 * head)
                    pe.wait_ge(at_out, 4 * head)
                for g in range(3):
                    v = qkvg[:, 12 + 2 * g + hh, :]
                    for r in range(4):
                        src = v[:, r * P:(r + 1) * P] if g == 0 else v[:, r::4]
                        last = pe.transpose(aux[:, 1 + g, r * P:(r + 1) * P], src, ident)
                    last.then_inc(at_vt, 1)

            scores(base)
            scores(base + 1)
            for u in range(base, base + 8):
                hh, r = (u // 4) % 2, u % 4
                if r == 0:
                    values(hh)
                pe.wait_ge(at_p, u + 1)
                if r == 0:
                    pe.wait_ge(at_vn, 3 * (2 * hp + hh) + 3)
                else:
                    pe.wait_ge(at_pt, u)
                for b in range(6):
                    last = pe.transpose(aux[:, 1 + b // 4, (b % 4) * P:(b % 4 + 1) * P],
                                        s_sb[:, u % 2, b * P:(b + 1) * P], ident)
                last.then_inc(at_t, 1)
                if u + 2 < base + 8:
                    scores(u + 2)
                pe.wait_ge(at_pt, u + 1)
                if hp == 0 and u == 1:
                    pe.wait_ge(mod_cols, 3)
                if r >= 2:
                    pe.wait_ge(at_out, u - 1)
                for b in range(6):
                    key = b if b < 4 else 4 * (b - 3) + r
                    last = pe.matmul(aux[:, 3 * (1 - u % 2), 0:P], vn[:, key, :],
                                     pt[:, u % 2, b * P:(b + 1) * P], start=(b == 0), stop=(b == 5))
                last.then_inc(at_o, 1)

        def attend_act(act, hp):
            base = 8 * hp

            def exps(u):
                act.wait_ge(at_nm, u + 1)
                act.activation(s_sb[:, u % 2, :], s_sb[:, u % 2, :], ACT.Exp, bias=nmx[:, u % 2:u % 2 + 1],
                               accum_out=lsum[:, u % 2:u % 2 + 1]).then_inc(at_e, 1)

            exps(base)
            exps(base + 1)
            for u in range(base, base + 8):
                if u % 4 == 0:
                    head = u // 4
                    if head > 0:
                        act.wait_ge(at_o, 4 * head)
                    for g in range(3):
                        act.wait_ge(at_vt, 3 * head + g + 1)
                        act.activation(vn[:, 4 * g:4 * g + 4, :], aux[:, 1 + g, :].rearrange("p (r d) -> p r d", d=P),
                                       ACT.Copy).then_inc(at_vn, 1)
                act.wait_ge(at_t, u + 1)
                if u >= 2:
                    act.wait_ge(at_o, u - 1)
                act.activation(pt[:, u % 2, :], bcast[:, 0:768], ACT.Copy).then_inc(at_pt, 1)
                if u + 2 < base + 8:
                    exps(u + 2)

        def attend_dve(dve, link, hp):
            base = 8 * hp

            def maxima(v):
                s, r = v % 2, v % 4
                dve.wait_ge(at_s, v + 1)
                if v >= 2:
                    dve.wait_ge(at_t, v - 1)
                dve.scalar_tensor_tensor(s_sb[:, s, 0:T], acc[:, s, 0:T], DH ** -0.5, mask[:, 3 - r:3 - r + T],
                                         ALU.mult, ALU.add)
                dve.scalar_tensor_tensor(s_sb[:, s, T:768], acc[:, s, T:768], DH ** -0.5, mask[:, 516:772],
                                         ALU.mult, ALU.add).then_inc(at_m, 1)
                dve.wait_ge(at_m, v + 1)
                dve.tensor_reduce(nmx[:, s:s + 1], s_sb[:, s, :], AX_X, ALU.max, negate=True).then_inc(at_nm, 1)

            def out(v):
                hh, r = (v // 4) % 2, v % 4
                dve.wait_ge(at_o, v + 1)
                dve.tensor_tensor(att[:, 2 * hp + hh, r::4], aux[:, 3 * (1 - v % 2), 0:P],
                                  qkvg[:, 2 * (N_ATT - 1) + hh, r::4], ALU.mult).then_inc(at_out, 1)

            maxima(base)
            maxima(base + 1)
            for u in range(base, base + 8):
                s = u % 2
                dve.wait_ge(at_e, u + 1)
                link(dve.reciprocal(rsum[:, s:s + 1], lsum[:, s:s + 1]))
                dve.tensor_scalar(s_sb[:, s, :], s_sb[:, s, :], rsum[:, s:s + 1], None, ALU.mult).then_inc(at_p, 1)
                if base < u < base + 7:
                    maxima(u + 1)
                if u > base:
                    out(u - 1)
            out(base + 7)

        def layer(pe, l, gemm, mv_reduce, norm_sums):
            X, XC = [(hxh, hxl, 0, T)], [(hxh, hxl, 0, T), (hch, hcl, T, TC)]
            base = C_L + l * N_L
            own = XC if l == 0 else X
            nj = 6 if l == 0 else 4
            norm_sums(n_mix[l], [(nsq2, T), (nsqc, TC)], ndg2)

            def modulated(q, segs):
                return lambda k: pe.wait_ge(n_out, q.t + segs * (k + 1))

            for j in range(N_WIN):
                gemm(base + j, j % 2, XC if l == 0 or j in (3, 4) else X, ready=None if j else modulated(n_mix[l], 2))
                if j == 5:
                    for c in range(2):
                        pe.wait_ge(acc_free[c], base + 4)
                    for b, src in enumerate((qT, kT)):
                        for c in range(2):
                            last = pe.matmul(aux[:, 2 * b + c, :], perm, src[:, c, 0:T], start=True, stop=True)
                    last.then_inc(rot, 1)
                if j == 7:
                    pe.wait_ge(roped, 4 * l + 4)
                    for i in range(6):
                        for c in range(2):
                            last = pe.transpose(auxf[:, i * GW + c * P:i * GW + (c + 1) * P],
                                                vT[:, c, i * P:(i + 1) * P], ident)
                    last.then_inc(v_t, 1)
            for c in range(2):
                pe.wait_ge(acc_free[c], base + N_WIN)
            flat = acc[:].rearrange("p a b -> p (a b)")

            def ln(q, src, cuts):
                for c in range(2):
                    for o, so, w in cuts:
                        last = pe.matmul(acc[:, 0, o:o + w], avg, src[:, c, so:so + w], start=(c == 0), stop=(c == 1),
                                         skip_group_check=True)
                last.then_inc(m_mean, 1)
                pe.wait_ge(m_sq, 2 * q + 2)
                for j in range(nj):
                    for c in range(2):
                        last = pe.matmul(ps_st[:, j:j + 1], sqm[:, c, j * P:(j + 1) * P], ones[:, 0:1],
                                         start=(c == 0), stop=(c == 1))
                last.then_inc(m_st, 1)
                pe.wait_ge(m_dg, q + 1)
                for j in range(nj):
                    last = pe.matmul(bcast[:, j * P:(j + 1) * P], ones, ndm[:, j, :], start=True, stop=True)
                last.then_inc(m_bc, 1)

            pe.wait_ge(v_nat, 3 * l + 3)
            pe.wait_ge(conv_step, CONV_STEPS * (l + 1))
            ln(2 * l, aconv, [(0, 0, T), (T, T + 30, TC)] if l == 0 else [(0, 0, T)])
            ln(2 * l + 1, svg, [(0, 0, T), (T, T, TC)] if l == 0 else [(0, 0, T)])
            pe.wait_ge(m_fin, 4 * l + 4)
            for j in range(nj):
                for c in range(2):
                    last = pe.transpose(flat[:, j * GW + c * P:j * GW + (c + 1) * P],
                                        svg[:, c, j * P:(j + 1) * P], ident)
            last.then_inc(s_t, 1)
            pe.wait_ge(s_nat, (nj // 2) + 3 * l)
            pe.wait_ge(ld_sg, 32 * (l + 1))
            for g in range(4):
                half = 64 * (g % 2)
                for j in range(nj):
                    last = pe.matmul(acc[half:half + 64, g // 2, j * P:(j + 1) * P],
                                     snat[:, j, 64 * g:64 * g + 64], wsT[:, g, :], start=True, stop=True)
            last.then_inc(s_mix, 1)
            pe.wait_ge(s_out, 2 * l + 2)
            units = [(h, j) for h in range(4) for j in range(nj)]
            u0 = 24 * l

            def build(h):
                for n, (hi, lo, sh, sl, w0) in enumerate(2 * [(hxh, qlo, 0, 1, 0)] + 2 * [(hxl, klo, 5, 3, 1)]):
                    i = n % 2
                    if n < 2:
                        if h > 0:
                            pe.wait_ge(q_e, 2 * (u0 + nj * h - 1) + i + 1)
                    else:
                        pe.wait_ge((st_act, st_dve)[i], 2 * (4 * l + h) + 1)
                    e = (2 * (h % 2) + i) * SEL
                    for o, w, hx_ in ((0, T, hi), (T, TC, (hch, hcl)[w0])):
                        if w0 == 0 and o and l:
                            continue
                        pe.matmul(acc[:, i, o:o + w], selr[:, e + 32 * sh:e + 32 * sh + P], hx_[:, 2 + h // 2, :],
                                  start=True, stop=False)
                        last = pe.matmul(acc[:, i, o:o + w], selr[:, e + 32 * sl:e + 32 * sl + P],
                                         lo[:, h // 2, o:o + w], start=False, stop=True)
                    last.then_inc(st_ps, 1)

            def scores(u):
                h, j = units[u]
                if j == 0:
                    build(h)
                for i in range(2):
                    if j == 0:
                        pe.wait_ge((st_act, st_dve)[i], 2 * (4 * l + h) + 2)
                        pe.wait_ge((st_act, st_dve)[1 - i], 2 * (4 * l + h) + 2)
                    else:
                        pe.wait_ge(q_e, 2 * (u0 + u - 1) + i + 1)
                    st = stack[h % 2]
                    for o, w in ((0, T), (T, TC)) if j < 4 else ((T, TC),):
                        last = pe.matmul(acc[:, i, o:o + w], st[:, i, j * P:(j + 1) * P], st[:, 2 + i, o:o + w],
                                         start=True, stop=True)
                    last.then_inc(q_s, 1)

            pe.wait_ge(sel_ok, l + 1)
            pe.wait_ge(qk_lo, l + 1)
            scores(0)
            scores(1)
            for u, (h, j) in enumerate(units):
                first = 0 if j < 4 else 4
                pe.wait_ge(q_w, u0 + u + 1)
                if u > 0:
                    pe.wait_ge(q_pt, u0 + u)
                for b in range(first, 6):
                    last = pe.transpose(bcast[:, b * P:(b + 1) * P], prob[:, u % 2, 0, b * P:(b + 1) * P], ident)
                last.then_inc(q_t, 1)
                if u + 2 < len(units):
                    scores(u + 2)
                pe.wait_ge(q_pt, u0 + u + 1)
                if u >= 2:
                    pe.wait_ge(q_on, u0 + u - 1)
                for b in range(first, 6):
                    last = pe.matmul(aux[:, 3 * (1 - u % 2), 0:64], ptd[:, u % 2, b * P:(b + 1) * P],
                                     vnat[:, b, 64 * h:64 * h + 64], start=(b == first), stop=(b == 5))
                last.then_inc(q_o, 1)
            pe.wait_ge(o_n, l + 1)
            for j in range(nj):
                for c in range(2):
                    last = pe.transpose(acc[:, c, j * P:(j + 1) * P], onat[:, j, c * P:(c + 1) * P], ident)
            last.then_inc(o_t, 1)
            base += N_WIN
            pe.wait_ge(y_lo, KT * (l + 1))
            with pe.Fori(0, N_WOUT // 2) as i:
                for s in range(2):
                    gemm(2 * i + s + base, s, own)
            norm_sums(n_ff[l], [(nsq2, T), (nsqc, TC)] if l == 0 else [(nsq2, T)], ndg2)
            base += N_WOUT
            hid = [(fxh, fxl, 0, T), (fch, fcl, T, TC)] if l == 0 else [(fxh, fxl, 0, T)]
            with pe.Fori(0, NFB) as b:
                for kind in range(2):
                    for i in range(2):
                        for s in range(2):
                            n = 8 * b + (base + 4 * kind + 2 * i + s)
                            last = 4 * kind + 2 * i + s
                            ready = None
                            if last == 0:
                                ready = modulated(n_ff[l], len(own))
                            if last == 4:
                                ready = lambda k: pe.wait_ge(f_lo, KT * b + (KT * NFB * l + k + 1))
                            gemm(n, s, hid if kind else own, ready=ready)
                            if l == 0 and last in FF_SUMS:
                                mv_reduce(b, 3, FF_SUMS.index(last), G1 + G2)

        def layer_act(act, l, split, norm_squares, norm_root, norm_modulate2):
            base = C_L + l * N_L
            two = l == 0
            wx = TX if two else T
            nj = wx // P
            if l == 0:
                act.wait_ge(ld_ctx, 16)
                act.wait_ge(n_bc, n_post.n + 1)
                norm_squares(cT, nsqc)
                for k in range(KT):
                    act.wait_ge(x_done, k + 1)
                    act.activation(nsq2[:, k, :], xT[:, k, :], ACT.Square).then_inc(n_sq, 1)
            else:
                act.wait_ge(acc_ready[1], base)
                for k in range(KT):
                    act.wait_ge(acc_free[k % 2], base - 4 + k // 2 + 1)
                    act.activation(nsq2[:, k, :], xT[:, k, :], ACT.Square).then_inc(n_sq, 1)
                    act.activation(nsqc[:, k, :], cT[:, k, :], ACT.Square).then_inc(n_sq, 1)
            act.wait_ge(lam_s, l + 1)
            act.activation(lam_x, lam_p, ACT.Exp).then_inc(lam_e, 1)
            norm_root(n_mix[l])
            act.wait_ge(mod_cols, l + 4)
            norm_modulate2(n_mix[l], l, 0, [(hxh, 0, T, 0), (hch, T, TC, 1)])
            kinds = [(av, ACT.Copy), (sigt, ACT.Sigmoid), (qT, ACT.Copy), (kT, ACT.Copy), (vT, ACT.Copy),
                     (cx, ACT.Copy), (None, None), (bgt, ACT.Copy), (ug, ACT.Gelu_apprx_tanh),
                     (svg, ACT.Gelu_apprx_tanh)]
            for j, (dst, func) in enumerate(kinds):
                n = base + j
                wj = TX if two or j in (3, 4) else T
                if j == 4:
                    act.wait_ge(glu, 2 * l + 2)
                if j == 5:
                    act.wait_ge(cx_zero, l + 1)
                for c in range(2):
                    if dst is None:
                        continue
                    act.wait_ge(acc_ready[c], n + 1)
                    if j == 5:
                        for o, d, w in ((0, 1, T), (T, T + 3, TC))[:2 if two else 1]:
                            ins = act.activation(cx[:, c, d:d + w], acc[:, c, o:o + w], func)
                    elif j == 2 and two:
                        act.activation(dst[:, c, 0:T], acc[:, c, 0:T], func)
                        ins = act.activation(dst[:, c, T:TX], acc[:, c, T:TX], func, scale=QSCALE)
                    else:
                        ins = act.activation(dst[:, c, 0:wj], acc[:, c, 0:wj], func)
                    ins.then_inc(acc_free[c], 1)
                split(n + 2, n % 2, n // 2 + 1)
                if j == 8:
                    act.wait_ge(v_t, l + 1)
                    for i in range(3):
                        act.activation(vnat[:, 2 * i:2 * i + 2, :].rearrange("p a b -> p (a b)"),
                                       auxf[:, 512 * i:512 * i + 512], ACT.Copy).then_inc(v_nat, 1)
            flat = acc[:].rearrange("p a b -> p (a b)")

            def y_split(src, c, k, y):
                act.activation(hxh[:, k, :], src[:, c, 0:T], ACT.Copy).then_inc(y_hi, 1)
                if two:
                    act.activation(hch[:, k, :], src[:, c, T:TX], ACT.Copy).then_inc(y_hi, 1)

            def ln(q, src, func, g, b):
                for c in range(2):
                    act.wait_ge(m_cen, 2 * q + c + 1)
                    act.activation(sqm[:, c, 0:wx], src[:, c, 0:wx], ACT.Square).then_inc(m_sq, 1)
                act.wait_ge(m_var, q + 1)
                act.activation(sdc[:, 0:nj], varc[:, 0:nj], ACT.Sqrt).then_inc(m_sd, 1)
                for c in range(2):
                    act.wait_ge(m_t, 2 * q + c + 1)
                    act.activation(src[:, c, 0:wx], src[:, c, 0:wx], func, bias=vcol(b, c, 1),
                                   scale=vcol(g, c, 1)).then_inc(m_fin, 1)

            ln(2 * l, yca, ACT.Silu, f"lag{l}", f"lab{l}")
            act.wait_ge(m_fin, 4 * l + 2)
            for c in range(2):
                y_split(yca, c, c, c)
            act.wait_ge(roped, 4 * l + 4)
            for x_, ctx_, src in ((hxh, hch, qT), (hxl, hcl, kT)):
                act.activation(x_[:, 2:4, :], src[:, :, 0:T], ACT.Copy)
                ins = act.activation(ctx_[:, 2:4, :], src[:, :, T:TX], ACT.Copy) if two or src is kT else ins
            ins.then_inc(qk_hi, 1)
            ln(2 * l + 1, svg, ACT.Identity, f"sgg{l}", f"sgb{l}")
            act.wait_ge(s_t, l + 1)
            for j in range(nj // 2):
                act.activation(snat[:, 2 * j:2 * j + 2, :].rearrange("p a b -> p (a b)"),
                               flat[:, 512 * j:512 * j + 512], ACT.Copy).then_inc(s_nat, 1)
            for c in range(2):
                act.wait_ge(s_out, 2 * l + c + 1)
                y_split(ug, c, 4 + c, 2 + c)
            for c in range(2):
                act.wait_ge(d_out, 2 * l + c + 1)
                y_split(bgt, c, 6 + c, 4 + c)
            units = [(h, j) for h in range(4) for j in range(nj)]
            u0 = 24 * l

            act.wait_ge(ld_sel, 16 * (l + 1))
            act.activation(selr[:], sel[:], ACT.Copy).then_inc(sel_ok, 1)
            act.wait_ge(y_lo, KT * l + 6)

            def exps(u):
                o = 0 if units[u][1] < 4 else T
                h = units[u][0]
                if units[u][1] == 0:
                    for n in (0, 2):
                        act.wait_ge(st_ps, 4 * (4 * l + h) + n + 1)
                        w = T if l and n == 0 else TX
                        act.activation(stack[h % 2][:, n, 0:w], acc[:, 0, 0:w], ACT.Copy).then_inc(st_act, 1)
                if u == 0:
                    act.wait_ge(s_mix, l + 1)
                    act.wait_ge(m_bc, 2 * l + 2)
                    act.wait_ge(s_out, 2 * l + 2)
                if u >= 2:
                    act.wait_ge(q_t, u0 + u - 1)
                for i in range(2):
                    act.wait_ge(q_m, 2 * (u0 + u) + i + 1)
                    z = 2 * (u % 2) + i
                    act.activation(prob[:, u % 2, i, o:TX], acc[:, i, o:TX], ACT.Exp, bias=dnm[:, z:z + 1],
                                   accum_out=dls[:, z:z + 1]).then_inc(q_e, 1)

            exps(0)
            exps(1)
            for u, (h, j) in enumerate(units):
                o = 0 if j < 4 else T
                act.wait_ge(q_t, u0 + u + 1)
                if u >= 2:
                    act.wait_ge(q_o, u0 + u - 1)
                act.activation(ptd[:, u % 2, o:TX], bcast[:, o:TX], ACT.Copy).then_inc(q_pt, 1)
                if u + 2 < len(units):
                    exps(u + 2)
                act.wait_ge(q_o, u0 + u + 1)
                act.activation(onat[:, j, 64 * h:64 * h + 64], aux[:, 3 * (1 - u % 2), 0:64], ACT.Identity,
                               scale=drs[:, 2 * (u % 4):2 * (u % 4) + 1]).then_inc(q_on, 1)
            act.wait_ge(q_on, u0 + len(units))
            act.activation(osq[:, 0:nj, :], onat[:, 0:nj, :], ACT.Square).then_inc(o_sq, 1)
            act.wait_ge(o_var, l + 1)
            act.activation(osd[:, 0:4 * nj], oss[:, 0:4 * nj], ACT.Sqrt).then_inc(o_sd, 1)
            act.wait_ge(o_t, l + 1)
            for c in range(2):
                y_split(acc, c, 2 + c, 6 + c)
            base += N_WIN
            with act.Fori(0, N_WOUT // 2) as i:
                for s in range(2):
                    n = 2 * i + s + base
                    for c in range(2):
                        act.wait_ge(acc_free[c], n + 1)
                        act.activation(tile(nsq2, 4 * i + 2 * s + c), tile(xT, 4 * i + 2 * s + c), ACT.Square
                                       ).then_inc(n_sq, 1)
                        if two:
                            act.activation(tile(nsqc, 4 * i + 2 * s + c), tile(cT, 4 * i + 2 * s + c), ACT.Square
                                           ).then_inc(n_sq, 1)
                    split(n + 2, s, i + base // 2 + 1)
            norm_root(n_ff[l])
            norm_modulate2(n_ff[l], l, 1, [(hxh, 0, T, 0), (hch, T, TC, 1)][:2 if two else 1])
            base += N_WOUT

            def ff(b, end=False):
                for i in range(2):
                    for s in range(2):
                        n = 8 * b + (base + 2 * i + s)
                        for c in range(2):
                            t = 4 * i + 2 * s + c
                            f0 = KT * b + (KT * NFB * l + t)
                            act.wait_ge(acc_ready[c], n + 1)
                            act.wait_ge(f_sq, f0 + 1)
                            act.activation(relu[:, c, 0:wx], acc[:, c, 0:wx], ACT.Relu).then_inc(acc_free[c], 1)
                            act.wait_ge(acc_free[c], n + 1)
                            ins = act.activation(fxh[:, t, :], relu[:, c, 0:T], ACT.Square)
                            if two:
                                ins = act.activation(fch[:, t, :], relu[:, c, T:TX], ACT.Square)
                            ins.then_inc(f_hi, 1)
                        split(n + 2, s, 4 * b + (base // 2 + i + 1))
                for i in range(1 if end else 2):
                    for s in range(2):
                        split(8 * b + (base + 4 + 2 * i + s + 2), s, 4 * b + (base // 2 + 2 + i + 1))

            with act.Fori(0, NFB - l) as b:
                ff(b)
            if l == L2 - 1:
                ff(NFB - 1, end=True)

        def layer_dve(dve, link, l, split, norm_scale, norm_modulate2, modulation):
            base = C_L + l * N_L
            two = l == 0
            wx = TX if two else T
            nj = wx // P
            lam_init = 0.8 - 0.6 * math.exp(-0.3 * l)
            dve.wait_ge(ld_rows, 16 * (l + 1))
            for i in range(2):
                link(dve.tensor_tensor(scr[:, 32 * i:32 * i + 32], rows[:, 64 + 64 * i:96 + 64 * i],
                                       rows[:, 96 + 64 * i:128 + 64 * i], ALU.mult))
            dve.tensor_reduce(lam_p, scr.rearrange("p (i d) -> p i d", i=2), AX_X, ALU.add).then_inc(lam_s, 1)
            for i, g in enumerate(("n1g", "n2g")):
                o = 2 * KT * (3 * i + 1)
                ins = dve.scalar_tensor_tensor(coef[i], mod2[:, o:o + 2 * KT], 1.0, vcol(f"{g}{l}"), ALU.add, ALU.mult)
            ins.then_inc(mod_cols, 1)
            dve.wait_ge(lam_e, l + 1)
            link(dve.scalar_tensor_tensor(lamc, lam_x[:, 1:2], lam_init, lam_x[:, 0:1], ALU.subtract, ALU.subtract))
            norm_scale(n_mix[l], ndg2)
            norm_modulate2(n_mix[l], [(xT, hxh, hxl, 0, T), (cT, hch, hcl, T, TC)])
            dve.memset(gpad[:], 0.0)
            wc = XPA - 30 if two else T
            segs = [(0, 15, T), (T, T + 45, TC)][:2 if two else 1]
            def rotate():
                dve.wait_ge(ld_rope, 16 * (l + 1))
                dve.wait_ge(rot, l + 1)
                for b, (src, scale) in enumerate(((qT, QSCALE), (kT, 1.0))):
                    for c in range(2):
                        if b or c:
                            dve.wait_ge(roped, 4 * l + 2 * b + c)
                        dve.scalar_tensor_tensor(tmp[:, 0:T], aux[:, 2 * b + c, :], scale, rope[:, 1, :], ALU.mult, ALU.mult)
                        link(dve.scalar_tensor_tensor(src[:, c, 0:T], src[:, c, 0:T], scale, rope[:, 0, :],
                                                      ALU.mult, ALU.mult))
                        dve.tensor_tensor(src[:, c, 0:T], src[:, c, 0:T], tmp[:, 0:T], ALU.add).then_inc(roped, 1)

            def short_conv(c):
                wd = XPD - 2 if two else T
                w = [vcol(f"cdw{l}", 3 * c + tap, 1) for tap in range(3)]
                dve.wait_ge(acc_free[c], base + 8)
                if c:
                    dve.wait_ge(d_out, 2 * l + 1)
                link(dve.tensor_scalar(dconv[:, 0:wd], cx[:, c, 0:wd], w[0], None, ALU.mult))
                for tap in range(1, 3):
                    link(dve.scalar_tensor_tensor(dconv[:, 0:wd], cx[:, c, tap:tap + wd], w[tap],
                                                  dconv[:, 0:wd], ALU.mult, ALU.add))
                for o, d, w_ in [(0, 0, T), (T, T + 2, TC)][:2 if two else 1]:
                    ins = dve.tensor_tensor(bgt[:, c, o:o + w_], dconv[:, d:d + w_], bgt[:, c, o:o + w_], ALU.mult)
                ins.then_inc(d_out, 1)

            step = 0
            for j in range(N_WIN):
                n = base + j
                if j == 1:
                    link(dve.memset(sc1, 0.0))
                    for c in range(2):
                        dve.wait_ge(acc_free[c], n + 1)
                        for o, d, w in segs:
                            ins = dve.tensor_tensor(gpad[:, c, d:d + w], av[:, c, o:o + w], sigt[:, c, o:o + w], ALU.mult)
                        ins.then_inc(glu, 1)
                    dve.wait_ge(glu, 2 * l + 2)
                    dve.memset(cx[:], 0.0).then_inc(cx_zero, 1)
                if j == 6:
                    for c in range(2):
                        dve.wait_ge(acc_ready[c], n + 1)
                        for o, d, w in [(0, 1, T), (T, T + 3, TC)][:2 if two else 1]:
                            if c == 0 and o == 0:
                                dve.wait_ge(acc_free[1], n)
                            ins = dve.tensor_tensor(cx[:, c, d:d + w], acc[:, c, o:o + w], cx[:, c, d:d + w], ALU.mult)
                        ins.then_inc(acc_free[c], 1)
                if j >= 2:
                    for _ in range(min(8, CONV_STEPS - step)):
                        tap, c = step // 2, step % 2
                        w = vcol(f"caw{l}", c * TAPS_A + tap, 1)
                        if tap == 0:
                            ins = dve.tensor_scalar(aconv[:, c, 0:wc], gpad[:, c, 0:wc], w, vcol(f"cab{l}", c, 1),
                                                    ALU.mult, ALU.add)
                        else:
                            dve.wait_ge(conv_step, CONV_STEPS * l + step - 1)
                            ins = dve.scalar_tensor_tensor(aconv[:, c, 0:wc], gpad[:, c, tap:tap + wc], w,
                                                           aconv[:, c, 0:wc], ALU.mult, ALU.add)
                        ins.then_inc(conv_step, 1)
                        step += 1
                split(n + 2, n % 2)
                if j == 6:
                    rotate()
                if j >= 8:
                    short_conv(j - 8)
            assert step == CONV_STEPS

            def y_split(src, c, k, y):
                per = 2 if two else 1
                dve.wait_ge(y_hi, 2 * KT * l + per * (y + 1))
                ins = dve.tensor_tensor(hxl[:, k, :], src[:, c, 0:T], hxh[:, k, :].bitcast(F32), ALU.subtract)
                if two:
                    ins = dve.tensor_tensor(hcl[:, k, :], src[:, c, T:TX], hch[:, k, :].bitcast(F32), ALU.subtract)
                ins.then_inc(y_lo, 1)

            def ln(q, src, dst, cuts):
                dve.wait_ge(m_mean, q + 1)
                for c in range(2):
                    for o, so, w in cuts:
                        ins = dve.tensor_tensor(dst[:, c, o:o + w], src[:, c, so:so + w], acc[:, 0, o:o + w],
                                                ALU.subtract)
                    ins.then_inc(m_cen, 1)
                dve.wait_ge(m_st, q + 1)
                dve.tensor_scalar(varc[:, 0:nj], ps_st[:, 0:nj], 1.0 / GW, EPS, ALU.mult, ALU.add).then_inc(m_var, 1)
                dve.wait_ge(m_sd, q + 1)
                link(dve.reciprocal(rsc[:, 0:nj], sdc[:, 0:nj]))
                for j in range(nj):
                    ins = dve.tensor_scalar(ndm[:, j, :], ident, rsc[:, j:j + 1], None, ALU.mult)
                ins.then_inc(m_dg, 1)
                dve.wait_ge(m_bc, q + 1)
                for c in range(2):
                    dve.tensor_tensor(dst[:, c, 0:wx], dst[:, c, 0:wx], bcast[:, 0:wx], ALU.mult).then_inc(m_t, 1)

            ln(2 * l, aconv, yca, [(0, 0, T), (T, T + 30, TC)] if two else [(0, 0, T)])
            for c in range(2):
                y_split(yca, c, c, c)
            dve.wait_ge(qk_hi, l + 1)
            for x_, ctx_, src, lo in ((hxh, hch, qT, qlo), (hxl, hcl, kT, klo)):
                ins = dve.tensor_tensor(lo[:, :, 0:T], src[:, :, 0:T], x_[:, 2:4, :].bitcast(F32), ALU.subtract)
                if two or src is kT:
                    ins = dve.tensor_tensor(lo[:, :, T:TX], src[:, :, T:TX], ctx_[:, 2:4, :].bitcast(F32), ALU.subtract)
            ins.then_inc(qk_lo, 1)
            ln(2 * l + 1, svg, svg, [(0, 0, wx)])
            dve.wait_ge(s_mix, l + 1)
            for c in range(2):
                if c:
                    dve.wait_ge(s_out, 2 * l + 1)
                link(dve.tensor_tensor(tmp[:, 0:wx].rearrange("p (j q) -> p j q", q=P),
                                       acc[:, c, 0:wx].rearrange("p (j q) -> p j q", q=P),
                                       bsg[:, c:c + 1, :].to_broadcast([P, nj, P]), ALU.add))
                dve.tensor_tensor(ug[:, c, 0:wx], tmp[:, 0:wx], ug[:, c, 0:wx], ALU.mult).then_inc(s_out, 1)
            for c in range(2):
                y_split(ug, c, 4 + c, 2 + c)
            for c in range(2):
                y_split(bgt, c, 6 + c, 4 + c)
            units = [(h, j) for h in range(4) for j in range(nj)]
            u0 = 24 * l

            def maxima(u):
                h, j = units[u]
                o = 0 if j < 4 else T
                if j == 0:
                    for n in (1, 3):
                        dve.wait_ge(st_ps, 4 * (4 * l + h) + n + 1)
                        w = T if l and n == 1 else TX
                        dve.tensor_copy(stack[h % 2][:, n, 0:w], acc[:, 1, 0:w]).then_inc(st_dve, 1)
                for i in range(2):
                    z = 2 * (u % 2) + i
                    dve.wait_ge(q_s, 2 * (u0 + u) + i + 1)
                    dve.tensor_reduce(dnm[:, z:z + 1], acc[:, i, o:TX], AX_X, ALU.max, negate=True).then_inc(q_m, 1)

            dve.wait_ge(y_lo, KT * l + 6)
            maxima(0)
            maxima(1)
            for u, (h, j) in enumerate(units):
                o = 0 if j < 4 else T
                z, y = 2 * (u % 2), 2 * (u % 4)
                dve.wait_ge(q_e, 2 * (u0 + u) + 2)
                if u >= 4:
                    dve.wait_ge(q_on, u0 + u - 3)
                link(dve.reciprocal(drs[:, y:y + 2], dls[:, z:z + 2]))
                link(dve.scalar_tensor_tensor(drs[:, y + 1:y + 2], drs[:, y + 1:y + 2], lamc, dls[:, z:z + 1],
                                              ALU.mult, ALU.mult))
                p1, p2 = prob[:, u % 2, 0, o:TX], prob[:, u % 2, 1, o:TX]
                dve.scalar_tensor_tensor(p1, p2, drs[:, y + 1:y + 2], p1, ALU.mult, ALU.add).then_inc(q_w, 1)
                if 1 <= u < len(units) - 1:
                    maxima(u + 1)
            ng = 4 * nj
            dve.wait_ge(o_sq, l + 1)
            link(dve.tensor_reduce(oss[:, 0:ng], osq[:, 0:nj, :].rearrange("p j (h d) -> p (j h) d", h=4), AX_X, ALU.add))
            dve.tensor_scalar(oss[:, 0:ng], oss[:, 0:ng], 1.0 / 64, EPS, ALU.mult, ALU.add).then_inc(o_var, 1)
            dve.wait_ge(o_sd, l + 1)
            link(dve.reciprocal(ors[:, 0:ng], osd[:, 0:ng]))
            o3 = onat[:, 0:nj, :].rearrange("p j (h d) -> p (j h) d", h=4)
            link(dve.tensor_tensor(o3, o3, ors[:, 0:ng].rearrange("p (g o) -> p g o", o=1).to_broadcast([P, ng, 64]),
                                   ALU.mult))
            dve.scalar_tensor_tensor(o3, o3, 1.0 - lam_init,
                                     rows[:, 0:64].rearrange("p (o d) -> p o d", o=1).to_broadcast([P, ng, 64]),
                                     ALU.mult, ALU.mult).then_inc(o_n, 1)
            for c in range(2):
                y_split(acc, c, 2 + c, 6 + c)

            def residual(t, c, part):
                for dst, o, w, z in ((xT, 0, T, 0), (cT, T, TC, 1))[:2 if two else 1]:
                    g0 = mod2_0 + 2 * (3 * KT * part + 2 * KT) + z
                    x_ = tile(dst, t)
                    ins = dve.scalar_tensor_tensor(x_, acc[:, c, o:o + w], small[:, bass.ds(2 * t + g0, 1)], x_,
                                                   ALU.mult, ALU.add)
                ins.then_inc(acc_free[c], 1)

            base += N_WIN
            with dve.Fori(0, N_WOUT // 2) as i:
                for s in range(2):
                    n = 2 * i + s + base
                    for c in range(2):
                        dve.wait_ge(acc_ready[c], n + 1)
                        residual(4 * i + (2 * s + c), c, 0)
                    split(n + 2, s)
            norm_scale(n_ff[l], ndg2)
            norm_modulate2(n_ff[l], [(xT, hxh, hxl, 0, T), (cT, hch, hcl, T, TC)][:2 if two else 1])
            base += N_WOUT

            def ff_modulation(b, m_):
                if l == 0 and FF_MV[m_] is not None:
                    modulation(b, 3, FF_MV[m_] // 2, G1 + G2, range(4 * (FF_MV[m_] % 2), 4 * (FF_MV[m_] % 2) + 4))

            def ff(b, end=False):
                for i in range(2):
                    for s in range(2):
                        n = 8 * b + (base + 2 * i + s)
                        for c in range(2):
                            t = 4 * i + 2 * s + c
                            f0 = KT * b + (KT * NFB * l + t)
                            dve.wait_ge(acc_free[c], n + 1)
                            dve.tensor_tensor(fsq[:, c, 0:wx], relu[:, c, 0:wx], relu[:, c, 0:wx], ALU.mult
                                              ).then_inc(f_sq, 1)
                            dve.wait_ge(f_sq, f0 + 3)
                            dve.wait_ge(f_hi, f0 + 1)
                            ins = dve.tensor_tensor(fxl[:, t, :], fsq[:, c, 0:T], fxh[:, t, :].bitcast(F32), ALU.subtract)
                            if two:
                                ins = dve.tensor_tensor(fcl[:, t, :], fsq[:, c, T:TX], fch[:, t, :].bitcast(F32),
                                                        ALU.subtract)
                            ins.then_inc(f_lo, 1)
                        split(n + 2, s)
                        ff_modulation(b, 2 * i + s)
                for i in range(2):
                    for s in range(2):
                        n = 8 * b + (base + 4 + 2 * i + s)
                        for c in range(2):
                            dve.wait_ge(acc_ready[c], n + 1)
                            residual(4 * i + 2 * s + c, c, 1)
                        if not (end and i == 1):
                            split(n + 2, s)
                        ff_modulation(b, 4 + 2 * i + s)

            with dve.Fori(0, NFB - l) as b:
                ff(b)
            if l == L2 - 1:
                ff(NFB - 1, end=True)
            else:
                dve.wait_ge(mv_sum, N_G)
                for c in range(2):
                    dve.wait_ge(acc_free[c], C_L + N_L)
                link(dve.tensor_tensor(mod2, ps_mv, vcol("ada_b1"), ALU.add))

        @block.sync
        def _(sync):
            def load_mv(i, per, g0, k):
                n0 = KT * g0 + k
                if isinstance(i, int):
                    i, per, n0, g0 = 0, 0, KT * (per * i + g0) + k, per * i + g0
                k_used = (k - MV_RING) % KT
                g_used = g0 if k >= MV_RING else g0 - 1
                used = i * (KT * per) + (n0 - MV_RING + 1)
                if n0 >= MV_RING:
                    sync.wait_ge(mv_x, used)
                if g_used >= G1 and k_used >= KX:
                    sync.wait_ge(mv_c, used)
                sync.dma_start(mvr[:, k % MV_RING, :], mst[bass.ds(i * (KT * per) + n0, 1)].rearrange("o p f -> (o p) f")
                               ).then_inc(mv_loaded[k % MV_RING], 16)

            def load_w(n, s):
                sync.wait_ge(w_lo, n - 1)
                sync.dma_start(raw[s][:], wst[bass.ds(n, 1)].rearrange("o p f -> (o p) f")
                               ).then_inc(w_loaded[s], 16)

            for g in range(4):
                for k in range(KT):
                    load_mv(0, 0, g, k)
                if g in (1, 2):
                    sync.dma_start(raw[g - 1][:], wst[g - 1]).then_inc(w_loaded[g - 1], 16)

            def pair(i, t0):
                for s in range(2):
                    load_w(2 * i + (2 * t0 + 2 + s), s)
                    for k in range(4 * s, 4 * s + 4):
                        load_mv(i, 1, 4 + t0, k)

            with sync.Fori(0, 2) as i:
                pair(i, 0)
            pair(0, 2)
            with sync.Fori(0, G2 - 1) as i:
                pair(i, 3)
            with sync.Fori(G1 - 4 + G2 + 1, (C_L + N_WIN + N_WOUT) // 2 + 1) as i:
                for s in range(2):
                    load_w(2 * i + s, s)
            sync.wait_ge(y_lo, KT)
            with sync.Fori(0, NFB) as b:
                for m_ in range(8):
                    load_w(8 * b + (m_ + C_L + N_WIN + N_WOUT + 2), m_ % 2)
                    if FF_MV[m_] is not None:
                        for k in range(4 * (FF_MV[m_] % 2), 4 * (FF_MV[m_] % 2) + 4):
                            load_mv(b, 3, G1 + G2 + FF_MV[m_] // 2, k)
            with sync.Fori((C_L + N_L) // 2 + 1, N_CHUNKS // 2) as i:
                for s in range(2):
                    load_w(2 * i + s, s)
            sync.wait_ge(x_done, 2 * KT)
            sync.dma_start(out, xT[:]).then_inc(stored, 16)
            sync.wait_ge(stored, 16)

        @block.gpsimd
        def _(pool):
            def add_squares(q, segs, in_turn=True):
                order = [(k, j) for k in range(KT) for j in range(len(segs))]
                if not in_turn:
                    order = [(k, j) for j in reversed(range(len(segs))) for k in range(KT)]
                done = [0] * len(segs)
                ad = q.sq // KT * (KT - 1)
                for n, (k, j) in enumerate(order):
                    if k == 0:
                        continue
                    pool.wait_ge(n_sq, q.sq + n + 1)
                    if k > 1:
                        pool.wait_ge(n_ad, done[j])
                    pool.tensor_tensor(segs[j][:, 0, :], segs[j][:, 0, :], segs[j][:, k, :], ALU.add).then_inc(n_ad, 1)
                    ad += 1
                    done[j] = ad

            def modulation(i, per, add, first, prod):
                g0 = first + add
                for k in range(KX, KT):
                    s = k % MV_RING
                    pool.wait_ge(mv_loaded[s], i * (32 * per) + 16 * (2 * g0 + k // MV_RING + 1))
                    pool.wait_ge(mv_c, i * (KT * per) + (KT * g0 + (k if k > KX else 0)))
                    pool.tensor_tensor(prod[:], mvr[:, s, :], sc2[:, 2 * k + 1:2 * k + 2].to_broadcast([P, MW]), ALU.mult
                                       ).then_inc(mv_p, 1)
                    pool.wait_ge(mv_p, i * (KC * per) + (KC * (g0 - G1) + k - KX + 1))
                    if k == KX:
                        pool.wait_ge(mv_x, i * (KT * per) + (KT * g0 + KX))
                    pool.tensor_tensor(macc[:, 1, :], macc[:, 1, :], prod[:], ALU.add
                                       ).then_inc(mv_c, 1 if k > KX else KX + 1)

            pool.memset(mprod[0][:], 0.0).then_inc(mv_c, KT * G1)
            add_squares(n_pre, [nsq])
            modulation(0, 1, 0, G1, mprod[0])
            with pool.Fori(1, G2) as i:
                modulation(i, 1, 0, G1, mprod[0])
            pool.wait_ge(at_out, 16)
            pool.dma_start(rope[:], rop).then_inc(ld_rope, 16)
            pool.dma_start(rows[:], row[0]).then_inc(ld_rows, 16)
            pool.wait_ge(mxl_done, KT)
            pool.dma_start(cT[:], cin).then_inc(ld_ctx, 16)
            add_squares(n_post, [nsq])
            for l in range(L2):
                if l:
                    pool.wait_ge(mv_sum, N_G)
                    pool.dma_start(rows[:], row[l]).then_inc(ld_rows, 16)
                    pool.dma_start(rope[:], rop).then_inc(ld_rope, 16)
                pool.dma_start(wsT[:], sgw[l]).then_inc(ld_sg, 16)
                pool.dma_start(bsg[:], sgb[l]).then_inc(ld_sg, 16)
                add_squares(n_mix[l], [nsq2, nsqc], in_turn=(l > 0))
                pool.wait_ge(roped, 4 * l + 4)
                pool.dma_start(sel[:], seli).then_inc(ld_sel, 16)
                add_squares(n_ff[l], [nsq2, nsqc][:2 - l])
                if l == 0:
                    with pool.Fori(0, NFB) as b:
                        for j in range(3):
                            modulation(b, 3, j, G1 + G2, mprod[1])
            add_squares(n_fin, [nsq2])

        @block.tensor
        def _(pe):
            def gemm(n, s, rhs, first=False, ready=None):
                pe.wait_ge(w_hi, n + 1)
                pe.wait_ge(w_lo, n + 1)
                wh = whi[s][:].rearrange("p (k c f) -> p k c f", k=KT, f=P)
                wl = wlo[s][:].rearrange("p (k c f) -> p k c f", k=KT, f=P)
                steps = [(k, c) for k in range(KT) for c in range(2)] if ready else \
                    [(k, c) for c in range(2) for k in range(KT)]
                for k, c in steps:
                    if k == 0 and not first:
                        pe.wait_ge(acc_free[c], n)
                    if ready and c == 0:
                        ready(k)
                    for w, part in ((wh, 0), (wh, 1), (wl, 0)):
                        for r in rhs:
                            last = pe.matmul(acc[:, c, r[2]:r[2] + r[3]], w[:, k, c, :], r[part][:, k, :],
                                             start=(k == 0 and w is wh and part == 0),
                                             stop=(k == KT - 1 and w is wl))
                    if k == KT - 1:
                        last.then_inc(acc_ready[c], 1)

            def mv_reduce(i, per, add, first):
                g0 = first + add
                done = i * (KT * per) + KT * (g0 + 1)
                pe.wait_ge(mv_x, done)
                if first:
                    pe.wait_ge(mv_c, done)
                for t in range(4):
                    for v in range(2 if first else 1):
                        if first:
                            col = tile(ps_mv.rearrange("p (a b) -> p a b", b=2), i * (4 * per) + (4 * add + t))[:, v:v + 1]
                        else:
                            col = ps_mv[:, 4 * add + t:4 * add + t + 1]
                        last = pe.matmul(col, macc[:, v, t * P:(t + 1) * P], ones[:, 0:1], start=True, stop=True)
                last.then_inc(mv_sum, 1)

            def norm_sums(q, segs, dg):
                pe.wait_ge(n_ad, (q.sq // KT + len(segs)) * (KT - 1))
                blocks = [(sq, o) for sq, w in segs for o in range(0, w, P)]
                for j, (sq, o) in enumerate(blocks):
                    last = pe.matmul(ps_st[:, j:j + 1], sq[:, 0, o:o + P], ones[:, 0:1], start=True, stop=True)
                last.then_inc(n_st, 1)
                pe.wait_ge(n_dg, q.n + 1)
                for j in range(len(blocks)):
                    last = pe.matmul(bcast[:, j * P:(j + 1) * P], ones, dg[:, j, :], start=True, stop=True)
                last.then_inc(n_bc, 1)

            HX = [(hxh, hxl, 0, T)]
            pe.wait_ge(ld_small, N_SMALL)
            pe.wait_ge(silu_c, 1)
            for g in range(4):
                mv_reduce(0, 0, g, 0)
            norm_sums(n_pre, [(nsq, T)], ndg)
            for n in range(C_MRG):
                gemm(n, n % 2, HX, first=(n == 0), ready=None if n else lambda k: pe.wait_ge(n_out, n_pre.t + k + 1))
                if n == 2 or n == 4:
                    mv_reduce(0, 0, n // 2 + 3, 0)
                if n == 6:
                    pe.wait_ge(mod_cols, 2)
                    mv_reduce(0, 0, 0, G1)

            def merge(i):
                for s in range(2):
                    gemm(C_MRG + 2 * i + s, s, HX)
                    pe.wait_ge(g_loaded[s], 16 * i + 16)
                    if not (isinstance(i, int) and i == 0 and s == 0):
                        pe.wait_ge(lru_ri, 4 * i + 2 * s)
                    for g in range(2):
                        last = pe.matmul(aux[:, 1 + g, :], wgate[:, s, g * P:(g + 1) * P], tile(uc, 2 * i + s),
                                         start=True, stop=True)
                    last.then_inc(lru_ps, 1)
                    if s == 0:
                        mv_reduce(i, 1, 1, G1)

            merge(0)
            with pe.Fori(1, N_MRG // 2) as i:
                merge(i)
            pe.wait_ge(lru_lo, KT)
            with pe.Fori(0, N_PB // 2) as i:
                for s in range(2):
                    gemm(C_PB + 2 * i + s, s, [(bh, bl, 0, T)])
                    if s == 0:
                        mv_reduce(i, 1, 1 + N_MRG // 2, G1)
            for hp in range(2):
                with pe.Fori(0, N_ATT // 2) as i:
                    for s in range(2):
                        gemm(C_ATT + hp * N_ATT + 2 * i + s, s, HX)
                        if hp == 0 and s == 0:
                            mv_reduce(i, 1, 1 + (N_MRG + N_PB) // 2, G1)
                attend(pe, hp)
            pe.wait_ge(atl_done, 4)
            for j in range(N_PA):
                n = C_PA + j
                pe.wait_ge(w_hi, n + 1)
                pe.wait_ge(w_lo, n + 1)
                wh = whi[j][:].rearrange("p (k c f) -> p k c f", k=4, f=P)
                wl = wlo[j][:].rearrange("p (k c f) -> p k c f", k=4, f=P)
                for c in range(4):
                    if c < 2:
                        pe.wait_ge(acc_free[c], n)
                    else:
                        pe.wait_ge(pa_free, 2 * j + c - 1)
                    for k in range(4):
                        pe.matmul(acc[:, c % 2, 0:T], wh[:, k, c, :], ath[:, k, :], start=(k == 0), stop=False)
                        pe.matmul(acc[:, c % 2, 0:T], wh[:, k, c, :], atl[:, k, :], start=False, stop=False)
                        last = pe.matmul(acc[:, c % 2, 0:T], wl[:, k, c, :], ath[:, k, :], start=False,
                                         stop=(k == 3))
                    last.then_inc(pa_ready if c < 2 else acc_ready[c % 2], 1)
            pe.wait_ge(mxl_done, KT)
            with pe.Fori(0, N_WO // 2) as i:
                for s in range(2):
                    gemm(C_WO + 2 * i + s, s, HX)
            norm_sums(n_post, [(nsq, T)], ndg)
            for l in range(L2):
                layer(pe, l, gemm, mv_reduce, norm_sums)
            norm_sums(n_fin, [(nsq2, T)], ndg2)

        @block.scalar
        def _(act):
            act.dma_start(vecs[:], vec).then_inc(ld_vec, 16)
            act.dma_start(xT[:], xin).then_inc(ld_small, 16)
            act.dma_start(consts[:], cst).then_inc(ld_small, 16)
            act.dma_start(mask[:], msk).then_inc(ld_small, 16)
            for j in range(2):
                act.dma_start(wgate[:, j, :], gst[j]).then_inc(g_loaded[j], 16)

            def split(n, s, half, first=False):
                act.wait_ge(w_loaded[s], 16 * half + 16)
                if not first:
                    act.wait_ge(acc_ready[1], n - 1)
                act.activation(whi[s][:], raw[s][:], ACT.Copy).then_inc(w_hi, 1)

            def norm_squares(src, sq):
                for k in range(KT):
                    act.activation(sq[:, k, :], src[:, k, :], ACT.Square).then_inc(n_sq, 1)

            def norm_modulate2(q, l, part, segs):
                shift = lambda k, z: mod2[:, 2 * (3 * KT * part + k) + z:2 * (3 * KT * part + k) + z + 1]
                scale = lambda k, z: coef[part][:, 2 * k + z:2 * k + z + 1]
                i = 0
                for k in range(KT):
                    for hi, o, w, z in segs:
                        act.wait_ge(n_t, q.t + i + 1)
                        if k >= 2:
                            act.wait_ge(n_out, q.t + i - 2 * len(segs) + 1)
                        for dst in (nh2[:, k % 2, o:o + w], hi[:, k, :]):
                            act.activation(dst, nt2[:, k % 2, o:o + w], ACT.Identity,
                                           bias=shift(k, z), scale=scale(k, z)).then_inc(n_h, 1)
                        i += 1

            def norm_root(q):
                act.wait_ge(n_var, q.n + 1)
                act.activation(sdc[:, 0:q.w // P], varc[:, 0:q.w // P], ACT.Sqrt).then_inc(n_sd, 1)

            def norm_modulate(q, scale, shift, hi):
                for k in range(KT):
                    act.wait_ge(n_t, q.t + k + 1)
                    if k >= 2:
                        act.wait_ge(n_out, q.t + k - 1)
                    act.activation(nh_[:, k % 2, 0:q.w], nt_[:, k % 2, 0:q.w], ACT.Identity,
                                   bias=shift(k), scale=scale(k)).then_inc(n_h, 1)
                    act.activation(hi[:, k, :], nt_[:, k % 2, 0:q.w], ACT.Identity,
                                   bias=shift(k), scale=scale(k)).then_inc(n_h, 1)

            act.wait_ge(ld_vec, 16)
            act.activation(sc1, vcol("c"), ACT.Silu).then_inc(silu_c, 1)
            act.activation(sc2, vcol("cc"), ACT.Silu).then_inc(silu_c, 1)
            act.wait_ge(ld_small, N_SMALL)
            norm_squares(xT, nsq)
            for s in range(2):
                split(s, s, 0, first=True)
            act.activation(l_abs, vcol("lru"), ACT.Abs).then_inc(lru_e, 1)
            act.wait_ge(lru_e, 1)
            act.activation(l_e, l_abs, ACT.Exp, scale=-1.0).then_inc(lru_e, 1)
            norm_root(n_pre)
            act.wait_ge(mod_cols, 1)
            norm_modulate(n_pre, lambda k: a1[:, k:k + 1], lambda k: mod1[:, k:k + 1], hxh)
            with act.Fori(0, N_U // 2) as i:
                for s in range(2):
                    for c in range(2):
                        t = 2 * s + c
                        act.wait_ge(acc_ready[c], 2 * i + s + 1)
                        act.activation(tile(uc, 4 * i + t), acc[:, c, 0:T], ACT.Identity,
                                       bias=vecs[:, bass.ds(4 * i + (VOFF["conv_b"][0] + t), 1)],
                                       scale=vecs[:, bass.ds(16 * i + (VOFF["conv_w"][0] + 4 * t), 1)]
                                       ).then_inc(u_tap0, 1)
                    split(2 * i + s + 2, s, i + 1)
            act.preload_act_table(ACT.Silu)
            with act.Fori(0, N_GL // 2) as i:
                for s in range(2):
                    for c in range(2):
                        act.wait_ge(acc_ready[c], 2 * i + s + C_GL + 1)
                        act.activation(tile(sg, 4 * i + 2 * s + c), acc[:, c, 0:T], ACT.Silu
                                       ).then_inc(acc_free[c], 1)
                    split(2 * i + s + C_GL + 2, s, i + C_GL // 2 + 1)
            act.wait_ge(lru_sp, 1)
            def merge(i, end=False):
                for s in range(2):
                    j = 2 * i + s
                    for c in range(2):
                        act.wait_ge(acc_ready[c], j + C_MRG + 1)
                        act.activation(tile(gates, 4 * i + 2 * s + c), acc[:, c, 0:T], ACT.Sigmoid
                                       ).then_inc(acc_free[c], 1)
                    split(j + C_MRG + 2, s, i + C_MRG // 2 + 1)
                    act.wait_ge(lru_ps, j + 1)
                    for g, (dst, b) in enumerate(((r_, "b_rg"), (i_, "b_ig"))):
                        act.activation(dst, aux[:, 1 + g, :], ACT.Sigmoid,
                                       bias=vecs[:, bass.ds(j + VOFF[b][0], 1)]).then_inc(lru_ri, 1)
                    if not end:
                        act.dma_start(wgate[:, s, :], gst[bass.ds(j + 2, 1)].rearrange("o p f -> (o p) f")
                                      ).then_inc(g_loaded[s], 16)
                    act.wait_ge(lru_ri, 2 * j + 2)

                    act.activation(tau, r_, ACT.Tanh, scale=small[:, bass.ds(j + sp0, 1)]).then_inc(lru_ta, 1)
                    act.activation(a_, r_, ACT.Exp, scale=small[:, bass.ds(j + (sp0 + KT), 1)]).then_inc(lru_ta, 1)
                    act.wait_ge(lru_z, j + 1)
                    act.activation(z_, z_, ACT.Sqrt).then_inc(lru_sq, 1)
                    act.wait_ge(lru_out, j + 1)
                    act.activation(tile(bh, j), x_, ACT.Copy).then_inc(lru_hi, 1)
            with act.Fori(0, N_MRG // 2 - 1) as i:
                merge(i)
            merge(N_MRG // 2 - 1, end=True)
            with act.Fori(0, N_PB // 2) as i:
                for s in range(2):
                    split(2 * i + s + C_PB + 2, s, i + C_PB // 2 + 1)
            for hp in range(2):
                n0 = C_ATT + hp * N_ATT
                act.wait_ge(acc_ready[0], n0 + 1)
                with act.Fori(0, N_ATT // 2 - 1) as i:
                    for s in range(2):
                        n = 2 * i + s + n0
                        act.wait_ge(acc_ready[0], n + 1)
                        act.activation(tile(qkvg, 4 * i + 2 * s), acc[:, 0, 0:T], ACT.Copy).then_inc(acc_free[0], 1)
                        split(n + 2, s, i + n0 // 2 + 1)
                for s in range(2):
                    n = n0 + N_ATT - 2 + s
                    for c in range(2):
                        if s == 0 and c == 1:
                            continue
                        act.wait_ge(acc_ready[c], n + 1)
                        act.activation(qkvg[:, 2 * (N_ATT - 2 + s) + c, :], acc[:, c, 0:T],
                                       ACT.Silu if s else ACT.Copy).then_inc(acc_free[c], 1)
                    split(n + 2, s, n // 2 + 1)
                attend_act(act, hp)
            act.wait_ge(at_out, 16)
            for k in range(4):
                act.activation(ath[:, k, :], att[:, k, :], ACT.Copy).then_inc(ath_done, 1)
            for j in range(N_PA):
                for c in range(4):
                    t = 4 * j + c
                    act.wait_ge(mix_done, t + 1)
                    act.activation(hxh[:, t, :], mix[:, t, :], ACT.Copy).then_inc(mxh_done, 1)
                split(C_PA + j + 2, j, C_PA // 2 + 1)
            for j in range(N_WO):
                n = C_WO + j
                for c in range(2):
                    act.wait_ge(acc_ready[c], n + 1)
                    act.activation(nsq[:, 2 * j + c, :], acc[:, c, 0:T], ACT.Square).then_inc(n_sq, 1)
                split(n + 2, n % 2, n // 2 + 1)
            norm_root(n_post)
            for l in range(L2):
                layer_act(act, l, split, norm_squares, norm_root, norm_modulate2)
            act.wait_ge(acc_ready[1], N_CHUNKS)
            for k in range(KT):
                act.wait_ge(acc_free[k % 2], N_CHUNKS - 4 + k // 2 + 1)
                act.activation(nsq2[:, k, :], xT[:, k, :], ACT.Square).then_inc(n_sq, 1)
            norm_root(n_fin)

        @block.vector
        def _(dve):
            chain = Chain(dve, dve_step)
            link = chain.link

            def split(n, s):
                dve.wait_ge(w_hi, n + 1)
                dve.tensor_tensor(wlo[s][:], raw[s][:], whi[s][:].bitcast(F32), ALU.subtract).then_inc(w_lo, 1)

            def modulation(i, per, add, first, ks):
                g0 = first + add
                for k in ks:
                    s = k % MV_RING
                    dve.wait_ge(mv_loaded[s], i * (32 * per) + 16 * (2 * g0 + k // MV_RING + 1))
                    if k == 0:
                        if not (isinstance(i, int) and per * i + g0 == 0):
                            dve.wait_ge(mv_sum, i * per + g0)
                    else:
                        dve.wait_ge(mv_x, i * (KT * per) + (KT * g0 + k))
                    for v in range(2 if first and k < KX else 1):
                        c = sc2[:, 2 * k + v:2 * k + v + 1] if first else sc1[:, k:k + 1]
                        if k == 0:
                            ins = dve.tensor_scalar(macc[:, v, :], mvr[:, s, :], c, None, ALU.mult)
                        else:
                            ins = dve.scalar_tensor_tensor(macc[:, v, :], mvr[:, s, :], c, macc[:, v, :],
                                                           ALU.mult, ALU.add)
                    ins.then_inc(mv_x, 1)

            def norm_scale(q, dg):
                nj = q.w // P
                dve.wait_ge(n_st, q.n + 1)
                dve.tensor_scalar(varc[:, 0:nj], ps_st[:, 0:nj], 1.0 / D, EPS, ALU.mult, ALU.add).then_inc(n_var, 1)
                dve.wait_ge(n_sd, q.n + 1)
                link(dve.reciprocal(rsc[:, 0:nj], sdc[:, 0:nj]))
                for j in range(nj):
                    last = dve.tensor_scalar(dg[:, j, :], ident, rsc[:, j:j + 1], None, ALU.mult)
                last.then_inc(n_dg, 1)
                dve.wait_ge(n_bc, q.n + 1)

            def norm_modulate2(q, segs):
                i = 0
                for k in range(KT + 1):
                    for j, (src, hi, lo, o, w) in enumerate(segs):
                        if k < KT:
                            if k >= 2:
                                dve.wait_ge(n_h, 2 * (q.t + (k - 2) * len(segs) + j + 1))
                            dve.tensor_tensor(nt2[:, k % 2, o:o + w], src[:, k, :], bcast[:, o:o + w], ALU.mult
                                              ).then_inc(n_t, 1)
                    for j, (src, hi, lo, o, w) in enumerate(segs):
                        if k > 0:
                            dve.wait_ge(n_h, 2 * (q.t + (k - 1) * len(segs) + j + 1))
                            dve.tensor_tensor(lo[:, k - 1, :], nh2[:, (k - 1) % 2, o:o + w],
                                              hi[:, k - 1, :].bitcast(F32), ALU.subtract).then_inc(n_out, 1)

            def norm_modulate(q, src, hi, lo):
                for k in range(KT + 1):
                    if k < KT:
                        if k >= 2:
                            dve.wait_ge(n_h, 2 * (q.t + k - 1))
                        dve.tensor_tensor(nt_[:, k % 2, 0:q.w], src[:, k, :], aux[:, 1, 0:q.w], ALU.mult
                                          ).then_inc(n_t, 1)
                    if k > 0:
                        dve.wait_ge(n_h, 2 * (q.t + k))
                        dve.tensor_tensor(lo[:, k - 1, :], nh_[:, (k - 1) % 2, 0:q.w],
                                          hi[:, k - 1, :].bitcast(F32), ALU.subtract).then_inc(n_out, 1)

            for c in range(2):
                dve.memset(lam_p[:, c:c + 1], 0.0).then_inc(f_sq, 1)
            dve.wait_ge(silu_c, 2)
            for g in range(4):
                modulation(0, 0, g, 0, range(KT))
            for s in range(2):
                split(s, s)
            dve.wait_ge(lru_e, 2)
            link(dve.tensor_scalar(l_z2, l_e, 2.0, None, ALU.add))
            link(dve.reciprocal(l_z, l_z2))
            link(dve.tensor_tensor(l_z, l_z, l_e, ALU.mult))
            link(dve.tensor_tensor(l_z2, l_z, l_z, ALU.mult))
            link(dve.tensor_scalar(l_q, l_z2, 1.0 / 19, None, ALU.mult))
            for d in range(17, 1, -2):
                link(dve.scalar_tensor_tensor(l_q, l_q, 1.0 / d, l_z2, ALU.add, ALU.mult))
            link(dve.scalar_tensor_tensor(l_q, l_q, 1.0, l_z, ALU.add, ALU.mult))
            link(dve.tensor_scalar(l_m, vcol("lru"), -8.0, 0.0, ALU.mult, ALU.max))
            link(dve.scalar_tensor_tensor(sp, l_q, 16.0, l_m, ALU.mult, ALU.add))
            dve.tensor_scalar(nsp, sp, -1.0, None, ALU.mult).then_inc(lru_sp, 1)

            dve.wait_ge(mv_sum, 4)
            link(dve.tensor_tensor(mod1[:, 0:2 * KT], ps_mv[:, 0:2 * KT], vcol("b_mod", 0, 2 * KT), ALU.add))
            dve.scalar_tensor_tensor(a1, mod1[:, KT:2 * KT], 1.0, vcol("g_pre"), ALU.add, ALU.mult
                                     ).then_inc(mod_cols, 1)
            norm_scale(n_pre, ndg)
            norm_modulate(n_pre, xT, hxh, hxl)
            with chain.loop(N_U // 2, 8) as i:
                for s in range(2):
                    for c in range(2):
                        t = 2 * s + c
                        dve.wait_ge(u_tap0, 4 * i + t + 1)
                        for tap in range(1, 4):
                            o = tile(uc, 4 * i + t)[:, tap:T]
                            ins = dve.scalar_tensor_tensor(
                                o, acc[:, c, 0:T - tap], vecs[:, bass.ds(16 * i + (VOFF["conv_w"][0] + 4 * t + tap), 1)],
                                o, ALU.mult, ALU.add)
                            if tap < 3:
                                link(ins)
                            else:
                                ins.then_inc(acc_free[c], 1)
                    split(2 * i + s + 2, s)
                    modulation(i, 1, 4, 0, range(4 * s, 4 * s + 4))
            dve.wait_ge(mv_sum, G1)
            link(dve.tensor_tensor(mod1[:, 2 * KT:3 * KT], ps_mv[:, 2 * KT:3 * KT], vcol("b_mod", 2 * KT, KT), ALU.add))
            dve.tensor_tensor(r1, mod1[:, 2 * KT:3 * KT], vcol("g_post"), ALU.mult).then_inc(mod_cols, 1)
            with dve.Fori(0, N_GL // 2) as i:
                for s in range(2):
                    split(2 * i + s + C_GL + 2, s)
                    modulation(i, 1, 0, G1, range(4 * s, 4 * s + 4))
            with chain.loop(N_MRG // 2, 8) as i:
                for s in range(2):
                    j = 2 * i + s
                    split(j + C_MRG + 2, s)
                    dve.wait_ge(lru_ta, 2 * j + 2)
                    link(dve.tensor_tensor(z_, a_, a_, ALU.mult))
                    dve.scalar_tensor_tensor(z_, z_, 1.0, tau, ALU.add, ALU.mult).then_inc(lru_z, 1)
                    link(dve.tensor_tensor(x_, i_, tile(uc, j), ALU.mult))
                    dve.wait_ge(lru_sq, j + 1)
                    link(dve.tensor_tensor(x_, x_, z_, ALU.mult))
                    link(dve.tensor_tensor_scan(z_, a_, x_, 0.0, ALU.mult, ALU.add))
                    dve.tensor_tensor(x_, z_, tile(sg, j), ALU.mult).then_inc(lru_out, 1)
                    dve.wait_ge(lru_hi, j + 1)
                    dve.tensor_tensor(tile(bl, j), x_, tile(bh, j).bitcast(F32), ALU.subtract).then_inc(lru_lo, 1)
                    modulation(i, 1, 2, G1, range(4 * s, 4 * s + 4))
            with dve.Fori(0, N_PB // 2) as i:
                for s in range(2):
                    for c in range(2):
                        dve.wait_ge(acc_ready[c], 2 * i + s + C_PB + 1)
                        g = tile(gates, 4 * i + (KT + 2 * s + c))
                        dve.tensor_tensor(g, acc[:, c, 0:T], g, ALU.mult).then_inc(acc_free[c], 1)
                    split(2 * i + s + C_PB + 2, s)
                    modulation(i, 1, 2 + N_MRG // 2, G1, range(4 * s, 4 * s + 4))
            for hp in range(2):
                n0 = C_ATT + hp * N_ATT
                with dve.Fori(0, N_ATT // 2 - 1) as i:
                    for s in range(2):
                        n = 2 * i + s + n0
                        dve.wait_ge(acc_ready[1], n + 1)
                        dve.tensor_copy(tile(qkvg, 4 * i + 2 * s + 1), acc[:, 1, 0:T]).then_inc(acc_free[1], 1)
                        split(n + 2, s)
                        if hp == 0:
                            modulation(i, 1, 2 + (N_MRG + N_PB) // 2, G1, range(4 * s, 4 * s + 4))
                n = n0 + N_ATT - 2
                dve.wait_ge(acc_ready[1], n + 1)
                dve.tensor_copy(qkvg[:, 2 * (N_ATT - 2) + 1, :], acc[:, 1, 0:T]).then_inc(acc_free[1], 1)
                split(n + 2, 0)
                split(n + 3, 1)
                if hp == 0:
                    dve.wait_ge(mv_sum, G1 + G2)
                    dve.tensor_tensor(mod2, ps_mv, vcol("ada_b0"), ALU.add).then_inc(mod_cols, 1)
                attend_dve(dve, link, hp)
            for k in range(4):
                dve.wait_ge(ath_done, k + 1)
                dve.tensor_tensor(atl[:, k, :], att[:, k, :], ath[:, k, :].bitcast(F32), ALU.subtract
                                  ).then_inc(atl_done, 1)
            for j in range(N_PA):
                for c in range(4):
                    t = 4 * j + c
                    dve.wait_ge(pa_ready if c < 2 else acc_ready[c % 2], 2 * j + c + 1 if c < 2 else C_PA + j + 1)
                    ins = dve.tensor_tensor(nt_[:, t % 2, :], acc[:, c % 2, 0:T], gate_a[:, t, :], ALU.mult)
                    ins.then_inc(pa_free if c < 2 else acc_free[c % 2], 1)
                    dve.wait_ge(pa_free if c < 2 else acc_free[c % 2], 2 * j + c + 1 if c < 2 else C_PA + j + 1)
                    dve.tensor_tensor(mix[:, t, :], mix[:, t, :], nt_[:, t % 2, :], ALU.add).then_inc(mix_done, 1)
                    dve.wait_ge(mxh_done, t + 1)
                    dve.tensor_tensor(hxl[:, t, :], mix[:, t, :], hxh[:, t, :].bitcast(F32), ALU.subtract
                                      ).then_inc(mxl_done, 1)
                split(C_PA + j + 2, j)
            for j in range(N_WO):
                n = C_WO + j
                for c in range(2):
                    dve.wait_ge(n_sq, n_post.sq + 2 * j + c + 1)
                    dve.tensor_copy(o32[:, 2 * j + c, :], acc[:, c, 0:T]).then_inc(acc_free[c], 1)
                split(n + 2, n % 2)
            norm_scale(n_post, ndg)
            for k in range(KT):
                link(dve.tensor_tensor(nt_[:, k % 2, :], o32[:, k, :], aux[:, 1, :], ALU.mult))
                dve.scalar_tensor_tensor(xT[:, k, :], nt_[:, k % 2, :], r1[:, k:k + 1], xT[:, k, :],
                                         ALU.mult, ALU.add).then_inc(x_done, 1)
            for l in range(L2):
                layer_dve(dve, link, l, split, norm_scale, norm_modulate2, modulation)
            norm_scale(n_fin, ndg2)
            for k in range(KT):
                dve.scalar_tensor_tensor(xT[:, k, :], xT[:, k, :], vcol("final_g", k, 1), bcast[:, 0:T],
                                         ALU.mult, ALU.mult).then_inc(x_done, 1)


def _cols(a):
    return np.reshape(a, (-1, P)).T


def _chunk(w, kt):
    return np.reshape(w, (kt, P, -1)).transpose(1, 0, 2).reshape(P, -1)


def _columns(w, width):
    return [_chunk(w[:, c:c + width], w.shape[0] // P) for c in range(0, w.shape[1], width)]


def _groups(w):
    return [w[P * k:P * k + P, c:c + MW] for c in range(0, w.shape[1], MW) for k in range(KT)]


def layout(inp):
    w_in = inp["w_in"][0]
    att, u0 = 9 * 512 + 512, 9 * 512 + 512
    chunks = _columns(w_in[:, u0:], CW)
    chunks += _columns(inp["w_pb"][0], CW)
    for hp in range(2):
        for j in range(N_ATT):
            c = 512 * j + CW * hp
            chunks.append(_chunk(w_in[:, c:c + CW], KT))
    chunks += _columns(inp["w_pa"][0], 2 * CW)
    chunks += _columns(inp["w_o"][0], CW)
    mv = _groups(inp["w_mod"][0])
    for l in range(L2):
        parts = _columns(inp["w_in_2"][l], CW)
        chunks += [parts[j] for j in W_IN_ORDER]
        chunks += _columns(inp["w_out_2"][l], CW)
        for b in range(NFB):
            chunks += _columns(inp["mlp_w1_2"][l][:, b * D:(b + 1) * D], CW)
            chunks += _columns(inp["mlp_w2_2"][l][b * D:(b + 1) * D], CW)
        mv += _groups(inp["ada_w_2"][l])
    assert len(chunks) == N_CHUNKS and len(mv) == KT * N_G

    def pair(a, b):
        return np.stack([_cols(a), _cols(b)], 2).reshape(P, -1)

    v = {"c": _cols(inp["c"][0]), "cc": pair(inp["c_2"][0], inp["c_ctx_2"]), "b_mod": _cols(inp["b_mod"][0]),
         "g_pre": _cols(inp["g_pre"][0]),
         "conv_w": np.reshape(inp["conv_w"][0], (4, KT, P)).transpose(2, 1, 0).reshape(P, -1),
         "conv_b": _cols(inp["conv_b"][0]), "b_rg": _cols(inp["b_rg"][0]), "b_ig": _cols(inp["b_ig"][0]),
         "lru": _cols(inp["lru_lambda"][0]), "g_post": _cols(inp["g_post"][0]), "final_g": _cols(inp["final_g_2"])}
    for l in range(L2):
        g = {"ada_b": "ada_b_2", "n1g": "norm1_g_2", "n2g": "norm2_g_2"}
        for k, name in g.items():
            v[f"{k}{l}"] = pair(inp[name][l], inp[name][l])
        v[f"caw{l}"] = np.reshape(inp["conv_a_w_2"][l], (TAPS_A, 2, P)).transpose(2, 1, 0).reshape(P, -1)
        v[f"cdw{l}"] = np.reshape(inp["conv_d_w_2"][l], (3, 2, P)).transpose(2, 1, 0).reshape(P, -1)
        for k, name in {"cab": "conv_a_b_2", "lag": "ln_a_g_2", "lab": "ln_a_b_2", "sgg": "sg_ln_g_2",
                        "sgb": "sg_ln_b_2"}.items():
            v[f"{k}{l}"] = _cols(inp[name][l])
    vec = np.concatenate([v[n] for n, _ in VECS], 1)
    assert vec.shape == (P, NV)

    gst = np.zeros((KT, P, 2, P), np.float32)
    for j in range(KT):
        for b in range(2):
            s = slice(64 * b, 64 * b + 64)
            gst[j, s, 0, s] = inp["w_rg"][0, 2 * j + b]
            gst[j, s, 1, s] = inp["w_ig"][0, 2 * j + b]
    x = np.reshape(inp["x"][0].T, (KT, P, T)).transpose(1, 0, 2)
    c = np.reshape(inp["ctx_2"][0].T, (KT, P, TC)).transpose(1, 0, 2)
    return {"wst": np.stack(chunks), "mst": np.stack(mv), "vec": vec, "xin": x, "cin": c,
            "gst": gst.reshape(KT, P, 2 * P), **layer_inputs(inp), **tables()}


def layer_inputs(inp):
    rows, sgw, sgb = [], [], []
    for l in range(L2):
        r = np.concatenate([inp["subln_g_2"][l]] + [inp[f"lam_{n}_2"][l] for n in ("q1", "k1", "q2", "k2")])
        rows.append(np.broadcast_to(r, (P, 192)))
        sgw.append(inp["sg_w_2"][l].transpose(2, 0, 1))
        sgb.append(np.repeat(np.reshape(inp["sg_b_2"][l], (2, 2, P)), 64, axis=1).transpose(1, 0, 2))
    return {"row": np.stack(rows), "sgw": np.stack(sgw), "sgb": np.stack(sgb)}


def tables():
    ident = np.eye(P, dtype=np.float32)
    ones = np.ones((P, P), np.float32)
    f = np.arange(P)
    partner = np.where(f % 16 < 8, f + 8, f - 8)
    perm = np.zeros((P, P), np.float32)
    perm[partner, f] = np.where(f % 16 < 8, -1.0, 1.0)
    cst = np.concatenate([ident, ones, perm, np.full((P, P), 1.0 / GW, np.float32)], 1)
    i = np.arange(P)[:, None]
    dist = 4 * i - (np.arange(T + 3)[None, :] - 3)
    band = np.where((dist >= 0) & (dist <= 128), 0.0, NEG)
    j = np.arange(P)[None, :]
    g1 = np.where(j <= i, 0.0, NEG)
    g2 = np.where((j <= i) & ((i - j) % 4 == 0), 0.0, NEG)
    msk = np.concatenate([band, np.zeros((P, 1)), g1, g2], 1).astype(np.float32)
    tok = np.arange(T)
    inv = np.float32(10000.0) ** (-np.arange(0, 16, 2, dtype=np.float32) / np.float32(16))
    pos = np.where(f[:, None] % 32 < 16, tok[None, :] // 64, tok[None, :] % 64).astype(np.float32)
    angle = pos * inv[f % 8][:, None]
    sel = np.zeros((P, 4, 9, 32), np.float32)
    for v in range(4):
        for b in (0, 2, 4, 5, 8):
            sel[32 * v + np.arange(32), v, b, np.arange(32)] = 1.0
    return {"sel": sel.reshape(P, -1), "cst": cst, "msk": msk, "rop": np.stack([np.cos(angle), np.sin(angle)], 1).astype(np.float32)}


_INS = ["wst", "mst", "vec", "xin", "cin", "gst", "cst", "msk", "rop", "sel", "row", "sgw", "sgb"]


def kernel(**inputs):
    import concourse.bacc as bacc
    from concourse.bass_utils import run_bass_kernel_spmd

    nc = bacc.Bacc("TRN2", target_bir_lowering=False, num_devices=1)
    data = layout(inputs)
    arrays, args = {}, []
    for name in _INS:
        a = np.ascontiguousarray(data[name])
        arrays[f"in_{name}"] = a
        args.append(nc.dram_tensor(f"in_{name}", a.shape, mybir.dt.from_np(a.dtype), kind="ExternalInput").ap())
    out = nc.dram_tensor("out_x", (P, KT, T), F32, kind="ExternalOutput").ap()
    build(nc, *args, out)
    r = run_bass_kernel_spmd(nc, [arrays], core_ids=[0])
    got = r.results[0]["out_x"]
    return np.ascontiguousarray(got.transpose(1, 0, 2).reshape(D, T).T)[None]
```
